# Optimizing a Trainium2 kernel written in Bass

```python
import math
import jax, jax.numpy as jnp
from jax import lax
import numpy as np

D_MODEL = 1024
BATCH = 1
SEQ = 512
DEPTH = 1
DEC_BATCH = 1
DEC_SEQ = 64
PAST_LEN = 512

CHUNK = 64
Q_BLOCK = 128
EPS = 1e-6
R_HEADS = 4
R_DK = 128
R_DV = 2 * R_DK
ROPE_BASE = 10000.0
D_HEADS = 4
D_DH = 128
D_DV = 2 * D_DH
R_QK_W = R_HEADS * R_DK
R_V_W = R_HEADS * R_DV
D_QK_W = D_HEADS * 2 * D_DH
D_V_W = D_HEADS * D_DV
SPLITS = (R_QK_W, R_QK_W, R_V_W, R_V_W, D_QK_W, D_QK_W, D_V_W, D_MODEL, D_MODEL)
SPLIT_POINTS = tuple(int(s) for s in np.cumsum(SPLITS)[:-1])
IN_W = int(sum(SPLITS))
N_GROUPS = 4
EXP_PER_GROUP = 4
N_EXPERTS = N_GROUPS * EXP_PER_GROUP
TOP_K = 2
D_FF = 512

kernel_name = "hybrid_retention_diffattn_hmoe_stream_step"

F32 = jnp.float32

def rmsnorm(x, g):
    xf = x.astype(F32)
    y = xf * lax.rsqrt(jnp.mean(xf * xf, axis=-1, keepdims=True) + EPS)
    return (y * g.astype(F32)).astype(x.dtype)

def retention_log_gamma():
    return jnp.log1p(-jnp.exp2(-5.0 - jnp.arange(R_HEADS, dtype=F32)))

def rotary(x, pos):
    half = x.shape[-1] // 2
    inv = 1.0 / (ROPE_BASE ** jnp.linspace(0.0, 1.0, half, dtype=F32))
    ang = pos.astype(F32)[:, None] * inv[None, :]
    cos = jnp.cos(ang)[None, :, None, :]
    sin = jnp.sin(ang)[None, :, None, :]
    x1, x2 = x[..., :half], x[..., half:]
    return jnp.concatenate([x1 * cos - x2 * sin, x1 * sin + x2 * cos], axis=-1)

def project(h, w_in, pos, g_q, g_k):
    B, T, _ = h.shape
    z = jnp.einsum('btd,de->bte', h, w_in)
    rq, rk, rv, rg, dq, dk, dv, gr, gd = jnp.split(z, SPLIT_POINTS, axis=-1)
    rq = rotary(rq.reshape(B, T, R_HEADS, R_DK).astype(F32), pos)
    rk = rotary(rk.reshape(B, T, R_HEADS, R_DK).astype(F32), pos) * (R_DK ** -0.5)
    rv = rv.reshape(B, T, R_HEADS, R_DV).astype(F32)
    rq, rk, rv = (a.transpose(0, 2, 1, 3) for a in (rq, rk, rv))
    dq = rmsnorm(dq.reshape(B, T, D_HEADS, 2, D_DH), g_q)
    dk = rmsnorm(dk.reshape(B, T, D_HEADS, 2, D_DH), g_k)
    dv = dv.reshape(B, T, D_HEADS, D_DV)
    return rq, rk, rv, rg, dq, dk, dv, gr, gd

def retention_chunk(state, q, k, v, log_gamma):
    L = q.shape[2]
    idx = jnp.arange(L, dtype=F32)
    intra = jnp.exp(log_gamma[:, None, None] * jnp.abs(idx[:, None] - idx[None, :]))
    s = jnp.einsum('bhld,bhmd->bhlm', q, k) * intra[None]
    o = jnp.einsum('bhlm,bhmv->bhlv', s, v)
    inter = jnp.exp(log_gamma[:, None] * (idx[None, :] + 1.0))
    o = o + jnp.einsum('bhld,bhdv->bhlv', q, state) * inter[None, :, :, None]
    wk = jnp.exp(log_gamma[:, None] * (L - 1.0 - idx[None, :]))
    new_state = (state * jnp.exp(log_gamma * L)[None, :, None, None]
                 + jnp.einsum('bhld,bhlv->bhdv', k * wk[None, :, :, None], v))
    return new_state, o

def retention_prompt(q, k, v, log_gamma):
    B, H, T, _ = q.shape
    n_chunks = T // CHUNK

    def to_chunks(a):
        return a.reshape(B, H, n_chunks, CHUNK, a.shape[-1]).transpose(2, 0, 1, 3, 4)

    def step(s, qkv):
        qc, kc, vc = qkv
        return retention_chunk(s, qc, kc, vc, log_gamma)

    s0 = jnp.zeros((B, H, R_DK, R_DV), F32)
    s_fin, o = lax.scan(step, s0, (to_chunks(q), to_chunks(k), to_chunks(v)))
    o = o.transpose(1, 2, 0, 3, 4).reshape(B, H, T, R_DV)
    return o, s_fin

def retention_out(o, rg, g_ret, w_ret_o):
    B, H, T, _ = o.shape
    o = rmsnorm(o, g_ret).transpose(0, 2, 1, 3).reshape(B, T, R_V_W).astype(rg.dtype)
    return jnp.einsum('btv,vd->btd', jax.nn.silu(rg) * o, w_ret_o)

def diff_attend(q, k, v, lam, mask):
    s = jnp.einsum('bqhmd,bkhmd->bhmqk', q, k).astype(F32) * (D_DH ** -0.5)
    if mask is not None:
        s = jnp.where(mask[None, None, None], s, -jnp.inf)
    p = jax.nn.softmax(s, axis=-1)
    a = p[:, :, 0] - lam * p[:, :, 1]
    return jnp.einsum('bhqk,bkhv->bhqv', a, v.astype(F32))

def diff_attn_prompt(q, k, v, lam):
    B, T = q.shape[:2]
    n_blocks = T // Q_BLOCK
    qb = q.reshape(B, n_blocks, Q_BLOCK, D_HEADS, 2, D_DH).swapaxes(0, 1)
    key_chunk = jnp.arange(T) // CHUNK

    def block(args):
        qi, i = args
        q_chunk = (i * Q_BLOCK + jnp.arange(Q_BLOCK)) // CHUNK
        mask = key_chunk[None, :] <= q_chunk[:, None]
        return diff_attend(qi, k, v, lam, mask)

    o = lax.map(block, (qb, jnp.arange(n_blocks)))
    return o.transpose(1, 2, 0, 3, 4).reshape(B, D_HEADS, T, D_DV)

def diff_out(o, g_sub, lam_init, w_diff_o, dtype):
    B, H, T, _ = o.shape
    o = rmsnorm(o, g_sub) * (1.0 - lam_init)
    o = o.transpose(0, 2, 1, 3).reshape(B, T, D_V_W).astype(dtype)
    return jnp.einsum('btv,vd->btd', o, w_diff_o)

def gated_merge(x, y_r, y_d, gr, gd, w_out):
    m = jax.nn.sigmoid(gr) * y_r + jax.nn.sigmoid(gd) * y_d
    return x + jnp.einsum('btd,de->bte', m, w_out)

def hier_moe(h, w_group, b_group, w_expert, b_expert, w_gate, w_up, w_down):
    B, T, D = h.shape
    xt = h.reshape(B * T, D)
    xf = xt.astype(F32)
    g_logits = xf @ w_group.astype(F32) + b_group.astype(F32)
    g_prob = jax.nn.softmax(g_logits, axis=-1)
    g_idx = jnp.argmax(g_logits, axis=-1)
    g_w = jnp.take_along_axis(g_prob, g_idx[:, None], axis=-1)
    e_logits = (xf @ w_expert.astype(F32) + b_expert.astype(F32)).reshape(-1, N_GROUPS, EXP_PER_GROUP)
    e_sel = jnp.take_along_axis(e_logits, g_idx[:, None, None], axis=1)[:, 0]
    e_prob = jax.nn.softmax(e_sel, axis=-1)
    top_v, top_i = lax.top_k(e_prob, TOP_K)
    top_v = top_v / jnp.sum(top_v, axis=-1, keepdims=True)
    global_idx = g_idx[:, None] * EXP_PER_GROUP + top_i
    combine = jnp.sum(jax.nn.one_hot(global_idx, N_EXPERTS, dtype=F32) * (g_w * top_v)[..., None], axis=1)
    y = jnp.zeros((B * T, D), F32)
    for e in range(N_EXPERTS):
        he = jax.nn.silu(xt @ w_gate[e]) * (xt @ w_up[e])
        y = y + combine[:, e:e + 1] * (he @ w_down[e]).astype(F32)
    return y.reshape(B, T, D).astype(h.dtype)

def setup_inputs(seed: int = 0) -> dict:
    key = jax.random.key(seed)
    ks = jax.random.split(key, 32)
    nrm = lambda k, shape, scale: jax.random.normal(k, shape, F32) * scale
    gain = lambda k, shape: 1.0 + 0.02 * jax.random.normal(k, shape, F32)
    L = DEPTH
    return {
        "x_prompt": nrm(ks[0], (BATCH, SEQ, D_MODEL), 1.0),
        "x_sample": nrm(ks[1], (DEC_BATCH, DEC_SEQ, D_MODEL), 1.0),
        "cache_k": nrm(ks[2], (L, DEC_BATCH, PAST_LEN, D_HEADS, 2 * D_DH), 1.0),
        "cache_v": nrm(ks[3], (L, DEC_BATCH, PAST_LEN, D_HEADS, D_DV), 1.0),
        "state_ret": nrm(ks[4], (L, DEC_BATCH, R_HEADS, R_DK, R_DV), 1.0),
        "g_mix": gain(ks[5], (L, D_MODEL)),
        "w_in": nrm(ks[6], (L, D_MODEL, IN_W), D_MODEL ** -0.5),
        "g_q": gain(ks[7], (L, D_DH)),
        "g_k": gain(ks[8], (L, D_DH)),
        "lambda_q1": nrm(ks[9], (L, D_DH), 0.1),
        "lambda_k1": nrm(ks[10], (L, D_DH), 0.1),
        "lambda_q2": nrm(ks[11], (L, D_DH), 0.1),
        "lambda_k2": nrm(ks[12], (L, D_DH), 0.1),
        "g_ret": gain(ks[13], (L, R_DV)),
        "w_ret_o": nrm(ks[14], (L, R_V_W, D_MODEL), R_V_W ** -0.5),
        "g_sub": gain(ks[15], (L, D_DV)),
        "w_diff_o": nrm(ks[16], (L, D_V_W, D_MODEL), D_V_W ** -0.5),
        "w_out": nrm(ks[17], (L, D_MODEL, D_MODEL), D_MODEL ** -0.5),
        "g_ffn": gain(ks[18], (L, D_MODEL)),
        "w_group": nrm(ks[19], (L, D_MODEL, N_GROUPS), D_MODEL ** -0.5),
        "b_group": nrm(ks[20], (L, N_GROUPS), 0.01),
        "w_expert": nrm(ks[21], (L, D_MODEL, N_EXPERTS), D_MODEL ** -0.5),
        "b_expert": nrm(ks[22], (L, N_EXPERTS), 0.01),
        "w_gate": nrm(ks[23], (L, N_EXPERTS, D_MODEL, D_FF), D_MODEL ** -0.5),
        "w_up": nrm(ks[24], (L, N_EXPERTS, D_MODEL, D_FF), D_MODEL ** -0.5),
        "w_down": nrm(ks[25], (L, N_EXPERTS, D_FF, D_MODEL), D_FF ** -0.5),
    }

def reference(x_prompt, x_sample, cache_k, cache_v, state_ret, g_mix, w_in, g_q, g_k,
              lambda_q1, lambda_k1, lambda_q2, lambda_k2, g_ret, w_ret_o, g_sub, w_diff_o,
              w_out, g_ffn, w_group, b_group, w_expert, b_expert, w_gate, w_up, w_down):
    log_gamma = retention_log_gamma()
    xp, xs = x_prompt, x_sample
    Bp, Tp = xp.shape[:2]
    Bs, Ts = xs.shape[:2]
    pos_p = jnp.arange(Tp, dtype=jnp.int32)
    pos_s = PAST_LEN + jnp.arange(Ts, dtype=jnp.int32)
    kp_l, vp_l, sp_l, ks_l, vs_l, ss_l = [], [], [], [], [], []
    for l in range(DEPTH):
        lam_init = 0.8 - 0.6 * math.exp(-0.3 * l)
        lam = (jnp.exp(jnp.sum(lambda_q1[l].astype(F32) * lambda_k1[l].astype(F32)))
               - jnp.exp(jnp.sum(lambda_q2[l].astype(F32) * lambda_k2[l].astype(F32))) + lam_init)

        h = rmsnorm(xp, g_mix[l])
        rq, rk, rv, rg, dq, dk, dv, gr, gd = project(h, w_in[l], pos_p, g_q[l], g_k[l])
        o_r, s_fin = retention_prompt(rq, rk, rv, log_gamma)
        o_d = diff_attn_prompt(dq, dk, dv, lam)
        xp = gated_merge(xp, retention_out(o_r, rg, g_ret[l], w_ret_o[l]),
                         diff_out(o_d, g_sub[l], lam_init, w_diff_o[l], xp.dtype), gr, gd, w_out[l])
        xp = xp + hier_moe(rmsnorm(xp, g_ffn[l]), w_group[l], b_group[l], w_expert[l], b_expert[l],
                           w_gate[l], w_up[l], w_down[l])
        kp_l.append(dk.reshape(Bp, Tp, D_HEADS, 2 * D_DH).astype(x_prompt.dtype))
        vp_l.append(dv.astype(x_prompt.dtype))
        sp_l.append(s_fin.astype(x_prompt.dtype))

        h = rmsnorm(xs, g_mix[l])
        rq, rk, rv, rg, dq, dk, dv, gr, gd = project(h, w_in[l], pos_s, g_q[l], g_k[l])
        s_new, o_r = retention_chunk(state_ret[l].astype(F32), rq, rk, rv, log_gamma)
        k_all = jnp.concatenate([cache_k[l].reshape(Bs, -1, D_HEADS, 2, D_DH).astype(dk.dtype), dk], axis=1)
        v_all = jnp.concatenate([cache_v[l].astype(dv.dtype), dv], axis=1)
        o_d = diff_attend(dq, k_all, v_all, lam, None)
        xs = gated_merge(xs, retention_out(o_r, rg, g_ret[l], w_ret_o[l]),
                         diff_out(o_d, g_sub[l], lam_init, w_diff_o[l], xs.dtype), gr, gd, w_out[l])
        xs = xs + hier_moe(rmsnorm(xs, g_ffn[l]), w_group[l], b_group[l], w_expert[l], b_expert[l],
                           w_gate[l], w_up[l], w_down[l])
        ks_l.append(dk.reshape(Bs, Ts, D_HEADS, 2 * D_DH).astype(x_sample.dtype))
        vs_l.append(dv.astype(x_sample.dtype))
        ss_l.append(s_new.astype(x_sample.dtype))

    return (xp, xs, jnp.stack(kp_l), jnp.stack(vp_l), jnp.stack(sp_l),
            jnp.stack(ks_l), jnp.stack(vs_l), jnp.stack(ss_l))


_drawn_inputs = setup_inputs


def setup_inputs(seed=0):
    import zlib

    import numpy as np

    out = dict(_drawn_inputs(seed))
    spreads = {}
    factors = {'g_k': 2.703,
     'g_ret': 2.899,
     'g_sub': 7.526,
     'b_group': 18.273,
     'b_expert': 16.227,
     'g_ffn': 3.097}
    for name, (base, spread) in spreads.items():
        noise = np.random.default_rng([zlib.crc32(name.encode()), seed]).standard_normal(out[name].shape)
        drawn = base * np.exp(spread * noise) if base else spread * noise
        out[name] = __import__('jax').numpy.asarray(drawn.astype(out[name].dtype))
    for name, factor in factors.items():
        out[name] = (out[name] * factor).astype(out[name].dtype)
    return out
```

```python
import math
import numpy as np
import concourse.bass as bass
from concourse import mybir

P = 128
D_MODEL = 1024
PROMPT = 512
SAMPLE = 64
PAST = 512
CHUNK = 64
TT = 5
PT = PROMPT // P
ROWS = TT * P
REAL = PROMPT + SAMPLE
EPS = 1e-6
H = 4
DK = 128
DV = 256
IN_W = 8192
KC = D_MODEL // P
COLS = 512
NE, NG, EPG = 16, 4, 4
D_FF = 512
FK = D_FF // P
BLK = 2048
RAW, SPL = 6, 3
IN_CHUNKS = IN_W // COLS
OUT_CHUNKS = 3 * D_MODEL // COLS
CHUNKS = IN_CHUNKS + OUT_CHUNKS
BPC = D_MODEL * COLS // P // BLK
N0 = CHUNKS * BPC
EB = 6
PASS_BLOCKS = EB * NE
UNITS = H * TT
KEYS = PROMPT + PAST + SAMPLE
SC = DK ** -0.5
NEG = -1e30
HEAD_USES = 7
LAM_INIT = 0.8 - 0.6 * math.exp(0.0)
SINK = ROWS

SECTION = [("k", 4096, 0), ("k", 4608, 512), ("q", 3072, 0), ("q", 3584, 512), ("v", 5120, 0), ("v", 5632, 512),
           ("rq", 0, 0), ("rk", 512, 0), ("rv", 1024, 0), ("rv", 1536, 512), ("rg", 2048, 0), ("rg", 2560, 512),
           ("gr", 6144, 0), ("gr", 6656, 512), ("gd", 7168, 0), ("gd", 7680, 512)]

DVE_CHUNKS = [c for c, (kind, _, _) in enumerate(SECTION) if kind in ("k", "q", "rq", "rk")]

GAMMA = [1.0 - 2.0 ** (-5.0 - h) for h in range(H)]


def shape_constants():
    f = np.float32
    p = np.arange(P)
    tok = np.arange(ROWS).reshape(TT, P).T
    gen = np.concatenate([np.eye(P), (p[:, None] < p[None, :]), np.ones((P, P)), np.tile(p, (P, 1)),
                          tok + 1, tok < REAL, (SINK + 1 + p)[:, None]], axis=1).astype(f)
    inv = (f(1.0) / (f(10000.0) ** np.linspace(0.0, 1.0, DK // 2, dtype=f))).astype(f)
    ang = (tok.astype(f)[:, :, None] * inv[None, None, :]).astype(f).astype(np.float64)
    rot = np.stack([np.cos(ang), np.sin(ang), np.cos(ang) * SC, np.sin(ang) * SC], axis=1).astype(f)
    dec = np.zeros((P, H, COLS))
    inter = np.zeros((P, H, P))
    wk = np.zeros((P, TT, H))
    m, n = p[:, None], np.arange(COLS)[None, :]
    seen = (m // CHUNK) <= (n // CHUNK)
    for h, g in enumerate(GAMMA):
        apart = np.where((m // CHUNK) == (n // CHUNK), np.abs(n - m), n - m)
        dec[:, h] = np.where(seen, g ** np.where(seen, apart, 0).astype(np.float64), 0.0)
        inter[:, h] = g ** (p[None, :] + 1.0)
        for t in range(PT):
            wk[:, t, h] = g ** (PROMPT - 1.0 - (t * P + p))
        wk[:SAMPLE, PT, h] = g ** (SAMPLE - 1.0 - p[:SAMPLE])
    ret = np.concatenate([dec.reshape(P, -1), inter.reshape(P, -1), wk.reshape(P, -1)], axis=1).astype(f)
    hide = np.concatenate([np.where(p < CHUNK, NEG, 0.0), np.where(p >= CHUNK, 1.0, 0.0)])[None, :].astype(f)
    return {"c_gen": gen, "c_rot": rot.reshape(P, -1), "c_ret": ret, "c_hide": hide}


class Steps:

    def __init__(self, eng, sem):
        self.eng, self.sem, self.n, self.base = eng, sem, 0, 0

    def __call__(self, ins):
        self.n += 1
        ins.then_inc(self.sem, 1)
        self.eng.wait_ge(self.sem, self.base + self.n)


def build(nc, a, o):
    f32, f32r, u32, i32 = mybir.dt.float32, mybir.dt.float32r, mybir.dt.uint32, mybir.dt.int32
    ALU, ACT, AX = mybir.AluOpType, mybir.ActivationFunctionType, mybir.AxisListType

    end = [0]

    def at(name, shape, dt, offset):
        size = 4 * int(np.prod(shape[1:]))
        end[0] = offset + (size + 31) // 32 * 32
        assert end[0] <= nc.sbuf_top, (name, end[0])
        return nc.alloc_sbuf_tensor_at(name, shape, dt, offset=offset)

    def after(name, shape, dt):
        return at(name, shape, dt, end[0])

    raw = at("raw", [P, RAW, BLK], f32, (nc.sbuf_base + 31) // 32 * 32)
    w_hi = after("w_hi", [P, SPL, BLK], f32r)
    w_lo = after("w_lo", [P, SPL, BLK], f32r)
    BIG = end[0]
    s_hi = after("s_hi", [P, KC, ROWS], f32r)
    s_lo = after("s_lo", [P, KC, ROWS], f32r)
    gen = after("gen", [P, 4 * P + 2 * TT + 1], f32)
    ident, tri, ones, iota = (gen[:, i * P:(i + 1) * P] for i in range(4))
    tok_plus1 = gen[:, 4 * P:4 * P + TT]
    tok_valid = gen[:, 4 * P + TT:4 * P + 2 * TT]
    sink_plus1 = gen[:, 4 * P + 2 * TT:4 * P + 2 * TT + 1]
    gq, gk = after("gq", [P, DK], f32), after("gk", [P, DK], f32)
    gret, gsub = after("gret", [P, DV], f32), after("gsub", [P, DV], f32)
    r_bias = after("r_bias", [P, NG + NE], f32)
    lam = after("lam", [P, 4], f32)
    stat = after("stat", [P, 5, TT, H], f32)
    REGION = end[0]
    rot = at("rot", [P, 4, TT, DK // 2], f32, REGION)
    stage = after("stage", [P, 3, TT, COLS], f32)
    x_tok = after("x_tok", [P, TT, D_MODEL], f32)
    h_tok = after("h_tok", [P, 2, D_MODEL], f32)
    sq_tmp = at("sq_tmp", [P, COLS], f32, end[0] - 8192)
    rot_tmp = at("rot_tmp", [P, 4, H, DK // 2], f32, end[0])
    gmix = at("gmix", [P, D_MODEL], f32, BIG - 4 * BLK)
    kT = at("kT", [P, 2, 2, KEYS], f32, BIG)
    qT = after("qT", [P, 2, 2, ROWS], f32)
    prob = after("prob", [P, 2, 2, PAST + SAMPLE], f32)
    assert end[0] <= BIG + 40960
    od = at("od", [P, TT, D_MODEL], f32, REGION)
    ro = after("ro", [P, TT, D_MODEL], f32)
    FREE = end[0]
    k_tok = at("k_tok", [P, TT, DV], f32, REGION + 20480)
    kc_tok = after("kc_tok", [P, PT, DV], f32)
    q_tok = after("q_tok", [P, TT, DV], f32)
    v_tok = after("v_tok", [P, 2, TT, DV], f32)
    vc_tok = after("vc_tok", [P, 2, PT, DV], f32)
    aT = after("aT", [P, 2, TT, P], f32)
    sq_att = after("sq_att", [P, DV], f32)
    neg_max = after("neg_max", [P, UNITS, 2], f32)
    sums = after("sums", [P, UNITS, 2], f32)
    coef = after("coef", [P, UNITS, 2], f32)
    lam_in = after("lam_in", [P, 4, DK], f32)
    hide = after("hide", [1, 2 * P], f32)
    decay = at("decay", [P, H, COLS], f32, BIG)
    inter = after("inter", [P, H, P], f32)
    wk = after("wk", [P, TT, H], f32)
    rq_tok = after("rq_tok", [P, 2, TT, DK], f32)
    rk_tok = after("rk_tok", [P, 2, TT, DK], f32)
    rv_tok = after("rv_tok", [P, 2, TT, DV], f32)
    assert end[0] <= BIG + 40960
    st_in = at("st_in", [P, 2, DV], f32, FREE)
    rqT = after("rqT", [P, ROWS], f32)
    rkT = after("rkT", [P, ROWS], f32)
    ST_OFF = [0, 512, 896, 1152, 1280]
    sT = after("sT", [P, 1280 + P], f32)
    q_int = after("q_int", [P, P], f32)
    kw = after("kw", [P, TT, DK], f32)
    st_out = after("st_out", [P, 2, DV], f32)
    sq_ret = after("sq_ret", [P, DV], f32)
    gate = at("gate", [P, 2, TT, COLS], f32, FREE)
    gffn = after("gffn", [P, D_MODEL], f32)
    md, x2, h2 = od, ro, od
    h2T = at("h2T", [P, KC, ROWS], f32, BIG)
    w_r = after("w_r", [P, KC, NG + NE], f32)
    zero_rows = after("zero_rows", [P, D_MODEL], f32)
    assert end[0] <= BIG + 40960
    logit = at("logit", [P, TT, NG + NE], f32, FREE + 9216)
    r4 = after("r4", [P, 10, TT, 4], f32)
    r1 = after("r1", [P, 12, TT, 1], f32)
    r16 = after("r16", [P, 4, TT, NE], f32)
    prod, sel, wt, posm = (r16[:, i] for i in range(4))
    slot_rhs = after("slot_rhs", [P, TT, NE, 2], f32)
    onehot = after("onehot", [P, 2, TT, P], f32)
    slot_tmp = after("slot_tmp", [P, 3, NE], f32)
    slot_w = after("slot_w", [P, NE], f32)
    g_idx = after("g_idx", [P, NE], u32)
    s_idx = after("s_idx", [P, NE], u32)
    g_cur, s_cur = after("g_cur", [P, 1], u32), after("s_cur", [P, 1], u32)
    w_cur = after("w_cur", [P, 1], f32)
    cmax = after("cmax", [P, 8], f32)
    npass = after("npass", [1, 1], i32)
    assert end[0] <= FREE + 20480
    x_hi = at("x_hi", [P, KC, P], f32r, REGION)
    x_lo = after("x_lo", [P, KC, P], f32r)
    a_hi = after("a_hi", [P, FK, P], f32r)
    a_lo = after("a_lo", [P, FK, P], f32r)
    x_exp = after("x_exp", [P, D_MODEL], f32)
    silu = after("silu", [P, D_FF], f32)
    act_t = after("act_t", [P, D_FF], f32)
    y_exp = after("y_exp", [P, D_MODEL], f32)
    w_lo2 = after("w_lo2", [P, SPL, BLK], f32r)
    assert end[0] <= FREE + 9216
    w_hi2 = at("w_hi2", [P, SPL, BLK], f32r, BIG)

    ps = nc.alloc_psum_tensor("ps", [P, 8, COLS], f32)
    psf = ps[:, :, :].rearrange("p b c -> p (b c)")

    def scratch(name, rows, cols):
        return nc.dram_tensor(name, (rows, cols), f32, kind="Internal").ap()

    z = {"q": scratch("z_q", ROWS, D_MODEL), "rq": scratch("z_rq", ROWS, COLS), "rk": scratch("z_rk", ROWS, COLS),
         "rv": scratch("z_rv", ROWS, D_MODEL), "rg": scratch("z_rg", ROWS, D_MODEL),
         "gr": scratch("z_gr", ROWS, D_MODEL), "gd": scratch("z_gd", ROWS, D_MODEL),
         "k": o["k_new"], "v": o["v_new"]}
    h2_dram = scratch("h2_dram", ROWS, D_MODEL)
    y_dram = o["y"]

    def tiles(ap, c0, c1, t0=0, t1=TT):
        return ap[t0 * P:t1 * P, c0:c1].rearrange("(t p) c -> p t c", p=P)

    def sem(name):
        return nc.alloc_semaphore(name)

    raw_full = [sem(f"raw_full{s}") for s in range(RAW)]
    hi_ready, lo_ready, blocks_used = sem("hi_ready"), sem("lo_ready"), sem("blocks_used")
    consts_in = sem("consts_in")
    rot_in, ret_in, router_in = sem("rot_in"), sem("ret_in"), sem("router_in")
    x_in = [sem(f"x_in{t}") for t in range(TT)]
    x_padded, x_squared, ms_ready, rms_ready = sem("x_padded"), sem("x_squared"), sem("ms_ready"), sem("rms_ready")
    shi_ready, slo_ready = sem("shi_ready"), sem("slo_ready")
    act_step, dve_step, pool_step = sem("act_step"), sem("dve_step"), sem("pool_step")
    z_ready, z_evacuated, z_staged = sem("z_ready"), sem("z_evacuated"), sem("z_staged")
    stage_stored = [sem(f"stage_stored{i}") for i in range(3)]
    kq_in, lam_loaded = sem("kq_in"), sem("lam_loaded")
    v_in = [sem("v_in0"), sem("v_in1")]
    tr_ready, tr_evacuated = sem("tr_ready"), sem("tr_evacuated")
    lam_dots, lam_exps = sem("lam_dots"), sem("lam_exps")
    scores_ready, max_ready, exp_ready = sem("scores_ready"), sem("max_ready"), sem("exp_ready")
    mix_ready = sem("mix_ready")
    av_ready, o_squared, o_copied = sem("av_ready"), sem("o_squared"), sem("o_copied")
    ret_head_in = [sem("ret_head_in0"), sem("ret_head_in1")]
    rtr_ready, rtr_evacuated = sem("rtr_ready"), sem("rtr_evacuated")
    s_ready, s_decayed, kw_ready, qint_ready = sem("s_ready"), sem("s_decayed"), sem("kw_ready"), sem("qint_ready")
    ro_ready, ro_squared, ro_copied = sem("ro_ready"), sem("ro_squared"), sem("ro_copied")
    state_ready, state_evacuated, state_stored = sem("state_ready"), sem("state_evacuated"), sem("state_stored")
    src_ready, src_transposed = sem("src_ready"), sem("src_transposed")
    gate_in = [sem("gate_in0"), sem("gate_in1")]
    p_ready, p_evacuated = sem("p_ready"), sem("p_evacuated")
    h2_ready, h2_tr, h2_evac = sem("h2_ready"), sem("h2_tr"), sem("h2_evac")
    y_init, h2_stored, zero_ready = sem("y_init"), sem("h2_stored"), sem("zero_ready")
    logits_ready, route_act, route_dve = sem("logits_ready"), sem("route_act"), sem("route_dve")
    sel_ready, pos_ready, npass_ready = sem("sel_ready"), sem("pos_ready"), sem("npass_ready")
    onehot_ready, onehot_used, lists_ready = sem("onehot_ready"), sem("onehot_used"), sem("lists_ready")
    x_gathered, x_tr, xhi_ready, xlo_ready = sem("x_gathered"), sem("x_tr"), sem("xhi_ready"), sem("xlo_ready")
    silu_ready, act_ready = sem("silu_ready"), sem("act_ready")
    a_tr, ahi_ready, alo_ready = sem("a_tr"), sem("ahi_ready"), sem("alo_ready")
    y_evac, y_scattered, cur_ready = sem("y_evac"), sem("y_scattered"), sem("cur_ready")

    def chunk_block(n):
        c, half = divmod(n, BPC)
        if c < IN_CHUNKS:
            w, c0 = a["w_in"][0], SECTION[c][1]
        else:
            p, j = divmod(c - IN_CHUNKS, 2)
            w, c0 = a[("w_diff_o", "w_ret_o", "w_out")[p]][0], j * COLS
        return w[half * 512:(half + 1) * 512, c0:c0 + COLS].rearrange("(k p) c -> p k c", p=P)


    def raw_view(n, k):
        return raw[:, n % RAW, :].rearrange("p (k c) -> p k c", k=k)

    PASS0 = N0 - 2
    assert PASS0 % RAW == 0 and EB % RAW == 0 and RAW % SPL == 0 and PASS_BLOCKS % RAW == 0

    def number(j, i, q):
        return PASS0 + PASS_BLOCKS * j + EB * i + q

    def hi_of(q):
        return w_hi[:, q % SPL, :] if q % RAW < SPL or q < 0 else w_hi2[:, q % SPL, :]

    def lo_of(q):
        return w_lo[:, q % SPL, :] if q % RAW < SPL or q < 0 else w_lo2[:, q % SPL, :]

    def split_hi(act, j, i, q):
        n = number(j, i, q)
        act.wait_ge(raw_full[q % RAW], 16 * (PASS0 // RAW + NE * j + i + q // RAW + 1))
        if isinstance(n, int) and n < N0 + 4:
            if n >= SPL:
                act.wait_ge(blocks_used, min(n - SPL + 1, N0))
        else:
            act.wait_ge(blocks_used, n - 2 * SPL + 1)
        nc.scalar.copy(hi_of(q), raw[:, q % RAW, :]).then_inc(hi_ready, 1)

    def split_lo(dve, j, i, q):
        dve.wait_ge(hi_ready, number(j, i, q) + 1)
        nc.vector.tensor_tensor(lo_of(q), raw[:, q % RAW, :], hi_of(q).bitcast(f32),
                                ALU.subtract).then_inc(lo_ready, 1)

    def wait_product(eng, ready, chunks_before, c, t):
        if t < TT - 1:
            eng.wait_ge(ready, (TT - 1) * (c - chunks_before) + t + 1)
        else:
            eng.wait_ge(blocks_used, BPC * (c + 1))

    def product(out, s_h, s_l, w_h, w_l, first, last):
        nc.tensor.matmul(out, s_h, w_h, start=first, stop=False)
        nc.tensor.matmul(out, s_l, w_h, start=False, stop=False)
        return nc.tensor.matmul(out, s_h, w_l, start=False, stop=last)

    def mix_uses(g):
        return 2 if g % TT == PT else 1

    def head_transposed(h):
        return HEAD_USES * (h + 1) + sum(mix_uses(g) for g in range(TT * h - 1))

    def unit_transposed(g):
        heads = min((g + 1) // TT, H - 1) + 1
        return HEAD_USES * heads + sum(mix_uses(u) for u in range(g + 1))

    def unit_width(t):
        return (t + 1) * P if t < PT else PAST + SAMPLE

    def scores_view(g):
        t = g % TT
        if t < PT:
            return ps[:, 2 * (g % 2):2 * (g % 2) + 2, 0:unit_width(t)]
        return psf[:, 0:4 * COLS].rearrange("p (m c) -> p m c", m=2)[:, :, 0:unit_width(t)]

    block = nc.Block()
    block.__enter__()

    @block.sync
    def _(sp):
        sp.dma_start(x_tok[:, 0, :], a["x_prompt"][0, 0:P, :]).then_inc(x_in[0], 16)
        sp.dma_start(raw_view(0, 4), chunk_block(0)).then_inc(raw_full[0], 16)
        for t in range(1, PT):
            sp.dma_start(x_tok[:, t, :], a["x_prompt"][0, t * P:(t + 1) * P, :]).then_inc(x_in[t], 16)
        sp.dma_start(x_tok[0:SAMPLE, PT, :], a["x_sample"][0]).then_inc(x_in[PT], 16)
        for n in range(1, N0):
            if n >= RAW:
                sp.wait_ge(lo_ready, n - RAW + 1)
            sp.dma_start(raw_view(n, 4), chunk_block(n)).then_inc(raw_full[n % RAW], 16)

        def expert_loads(base, i, q, kind, part):
            n = base + q
            sp.wait_ge(lo_ready, n - RAW + 1)
            w = a[kind][0]
            if kind == "w_down":
                src = w[bass.ds(i, 1), part * 256:(part + 1) * 256, :].rearrange("e (k p) c -> p (e k) c", p=P)
                dst = raw[:, q % RAW, :].rearrange("p (k c) -> p k c", k=2)
            else:
                src = w[bass.ds(i, 1), part * 512:(part + 1) * 512, :].rearrange("e (k p) c -> p (e k) c", p=P)
                dst = raw[:, q % RAW, :].rearrange("p (k c) -> p k c", k=4)
            sp.dma_start(dst, src).then_inc(raw_full[q % RAW], 16)

        def expert_body(base, i, up_gate=True, down=True):
            if up_gate:
                for q, (kind, part) in enumerate((("w_up", 0), ("w_up", 1), ("w_gate", 0), ("w_gate", 1))):
                    expert_loads(base, i, q, kind, part)
            if down:
                for part in range(2):
                    expert_loads(base, i - 1, 4 + part, "w_down", part)

        def expert_pass(first):
            for q, (kind, part) in enumerate((("w_up", 0), ("w_up", 1), ("w_gate", 0), ("w_gate", 1))):
                expert_loads(first - 2, 0, 2 + q, kind, part)
            with sp.Fori(1, NE) as i:
                expert_body(first - 2 + EB * i, i)
            for part in range(2):
                expert_loads(first - 2 + EB * NE, NE - 1, part, "w_down", part)

        expert_pass(N0)
        sp.wait_ge(npass_ready, 1)
        passes = sp.value_load(npass[0:1, 0:1], min_val=1, max_val=TT)
        with sp.If(passes > 1):
            with sp.Fori(1, passes) as j:
                expert_pass(N0 + PASS_BLOCKS * j)

    def store_states(pool, h):
        pool.wait_ge(state_evacuated, 2 * (h + 1))
        pool.dma_start(o["s_prompt"][h], st_out[:, 0, :]).then_inc(state_stored, 16)
        pool.dma_start(o["s_sample"][h], st_out[:, 1, :]).then_inc(state_stored, 16)

    @block.gpsimd
    def _(pool):
        own = Steps(pool, pool_step)
        dma = pool.dma_start
        dma(gmix[:, :], a["g_mix"][0].partition_broadcast(P)).then_inc(consts_in, 16)
        dma(gen[:, :], a["c_gen"]).then_inc(consts_in, 16)
        dma(rot[:, :, :, :], a["c_rot"].rearrange("p (a t c) -> p a t c", a=4, t=TT)).then_inc(rot_in, 16)
        dma(gq[:, :], a["g_q"][0].partition_broadcast(P)).then_inc(rot_in, 16)
        dma(gk[:, :], a["g_k"][0].partition_broadcast(P)).then_inc(rot_in, 16)
        dma(gret[:, :], a["g_ret"][0].partition_broadcast(P)).then_inc(rot_in, 16)
        dma(gsub[:, :], a["g_sub"][0].partition_broadcast(P)).then_inc(rot_in, 16)
        dma(r_bias[:, 0:NG], a["b_group"][0].partition_broadcast(P)).then_inc(rot_in, 16)
        dma(r_bias[:, NG:NG + NE], a["b_expert"][0].partition_broadcast(P)).then_inc(rot_in, 16)

        for c, (kind, _, c0) in enumerate(SECTION):
            if c in DVE_CHUNKS:
                pool.wait_ge(z_staged, DVE_CHUNKS.index(c) + 1)
            else:
                pool.wait_ge(z_evacuated, TT * (c + 1))
            if kind in "kv":
                dma(tiles(z[kind], c0, c0 + COLS, 0, PT), stage[:, c % 3, 0:PT, :]).then_inc(stage_stored[c % 3], 16)
                dma(z[kind][PROMPT:REAL, c0:c0 + COLS], stage[0:SAMPLE, c % 3, PT, :])\
                    .then_inc(stage_stored[c % 3], 16)
            else:
                dma(tiles(z[kind], c0, c0 + COLS), stage[:, c % 3, :, :]).then_inc(stage_stored[c % 3], 16)
        for s in range(3):
            pool.wait_ge(stage_stored[s], stored(IN_CHUNKS - 1, s))

        for n, name in enumerate(("lambda_q1", "lambda_k1", "lambda_q2", "lambda_k2")):
            dma(lam_in[:, n, :], a[name][0].partition_broadcast(P)).then_inc(lam_loaded, 16)
        dma(hide[:, :], a["c_hide"]).then_inc(lam_loaded, 16)
        for h in range(H):
            lo, up = h * DV, (h + 1) * DV
            if h >= 1:
                pool.wait_ge(tr_evacuated, head_transposed(h - 1))
            dma(k_tok[:, 0:PT, :], tiles(z["k"], lo, up, 0, PT)).then_inc(kq_in, 16)
            dma(k_tok[0:SAMPLE, PT, :], z["k"][PROMPT:REAL, lo:up]).then_inc(kq_in, 16)
            dma(kc_tok[:, :, :], a["cache_k"][0, 0, :, h, :].rearrange("(t p) c -> p t c", p=P)).then_inc(kq_in, 16)
            dma(q_tok[:, :, :], tiles(z["q"], lo, up)).then_inc(kq_in, 16)
            if h >= 2:
                pool.wait_ge(av_ready, TT * (h - 1))
            dma(v_tok[:, h % 2, 0:PT, :], tiles(z["v"], lo, up, 0, PT)).then_inc(v_in[h % 2], 16)
            dma(v_tok[0:SAMPLE, h % 2, PT, :], z["v"][PROMPT:REAL, lo:up]).then_inc(v_in[h % 2], 16)
            dma(vc_tok[:, h % 2, :, :], a["cache_v"][0, 0, :, h, :].rearrange("(t p) c -> p t c", p=P))\
                .then_inc(v_in[h % 2], 16)

        pool.wait_ge(o_copied, UNITS)
        pool.wait_ge(o_squared, UNITS)
        c_ret = a["c_ret"]
        dma(decay[:, :, :], c_ret[:, 0:H * COLS].rearrange("p (h c) -> p h c", h=H)).then_inc(ret_in, 16)
        dma(inter[:, :, :], c_ret[:, H * COLS:H * COLS + H * P].rearrange("p (h c) -> p h c", h=H)).then_inc(ret_in, 16)
        dma(wk[:, :, :], c_ret[:, H * COLS + H * P:].rearrange("p (t h) -> p t h", h=H)).then_inc(ret_in, 16)
        for h in range(H):
            if h >= 2:
                pool.wait_ge(state_evacuated, 2 * (h - 1))
            got = ret_head_in[h % 2]
            dma(rq_tok[:, h % 2, :, :], tiles(z["rq"], h * DK, (h + 1) * DK)).then_inc(got, 16)
            dma(rk_tok[:, h % 2, :, :], tiles(z["rk"], h * DK, (h + 1) * DK)).then_inc(got, 16)
            dma(rv_tok[:, h % 2, :, :], tiles(z["rv"], h * DV, (h + 1) * DV)).then_inc(got, 16)
            dma(st_in[:, h % 2, :], a["state_ret"][0, 0, h]).then_inc(got, 16)
            if h >= 1:
                store_states(pool, h - 1)
        store_states(pool, H - 1)
        pool.wait_ge(state_stored, 32 * H)
        pool.wait_ge(ro_squared, UNITS)

        dma(gffn[:, :], a["g_ffn"][0].partition_broadcast(P)).then_inc(router_in, 16)
        for n, kind in enumerate(("rg", "rg", "gd", "gd", "gr", "gr", "x", "x")):
            if n in (2, 3):
                pool.wait_ge(src_ready, 3 * TT)
            elif n >= 4:
                pool.wait_ge(p_evacuated, TT * (n - 3))
            c0, got = (n % 2) * COLS, gate_in[n % 2]
            if kind == "x":
                dma(gate[:, n % 2, 0:PT, :], tiles(a["x_prompt"][0], c0, c0 + COLS, 0, PT)).then_inc(got, 16)
                dma(gate[0:SAMPLE, n % 2, PT, :], a["x_sample"][0][:, c0:c0 + COLS]).then_inc(got, 16)
            else:
                dma(gate[:, n % 2, :, :], tiles(z[kind], c0, c0 + COLS)).then_inc(got, 16)

        pool.wait_ge(blocks_used, N0)
        dma(w_r[:, :, 0:NG], a["w_group"][0].rearrange("(k p) c -> p k c", p=P)).then_inc(router_in, 16)
        dma(w_r[:, :, NG:NG + NE], a["w_expert"][0].rearrange("(k p) c -> p k c", p=P)).then_inc(router_in, 16)
        pool.wait_ge(p_evacuated, TT * OUT_CHUNKS)
        dma(tiles(y_dram, 0, D_MODEL), x2[:, :, :]).then_inc(y_init, 16)
        pool.wait_ge(zero_ready, 1)
        dma(y_dram[SINK:SINK + P, :], zero_rows[:, :]).then_inc(y_init, 16)
        pool.wait_ge(h2_ready, TT)
        dma(tiles(h2_dram, 0, D_MODEL), h2[:, :, :]).then_inc(h2_stored, 16)
        pool.wait_ge(h2_stored, 16)
        pool.wait_ge(y_init, 32)

        def gather(i, e):
            own(nc.gpsimd.tensor_copy(g_cur[:, :], g_idx[:, bass.ds(i, 1)]))
            pool.indirect_dma_start(out=x_exp[:, :], out_offset=None, in_=h2_dram,
                                    in_offset=bass.IndirectOffsetOnAxis(ap=g_cur[:, :], axis=0))\
                .then_inc(x_gathered, 16)

        def scatter(i, e):
            own(nc.gpsimd.tensor_copy(s_cur[:, :], s_idx[:, bass.ds(i, 1)]))
            nc.gpsimd.tensor_copy(w_cur[:, :], slot_w[:, bass.ds(i, 1)]).then_inc(cur_ready, 1)
            pool.wait_ge(y_evac, 2 * (e + 1))
            pool.indirect_dma_start(out=y_dram, out_offset=bass.IndirectOffsetOnAxis(ap=s_cur[:, :], axis=0),
                                    in_=y_exp[:, :], in_offset=None, compute_op=ALU.add).then_inc(y_scattered, 16)
            pool.wait_ge(y_scattered, 16 * (e + 1))

        def expert_pass(j):
            e0 = NE * j
            pool.wait_ge(lists_ready, j + 1)
            gather(0, e0)
            pool.wait_ge(x_tr, 2 * (e0 + 1))
            gather(1, e0 + 1)
            for i in range(1, NE - 1):
                pool.wait_ge(x_tr, 2 * (e0 + i + 1))
                gather(i + 1, e0 + i + 1)
                if i >= 2:
                    scatter(i - 2, e0 + i - 2)
            scatter(NE - 3, e0 + NE - 3)
            scatter(NE - 2, e0 + NE - 2)
            scatter(NE - 1, e0 + NE - 1)

        expert_pass(0)
        pool.wait_ge(npass_ready, 1)
        passes = pool.value_load(npass[0:1, 0:1], min_val=1, max_val=TT)
        for j in range(1, TT):
            with pool.If(passes > j):
                expert_pass(j)

    @block.scalar
    def _(act):
        own = Steps(act, act_step)
        roots = [0]

        def root():
            roots[0] += 1
            act.wait_ge(ms_ready, roots[0])
            nc.scalar.activation(stat[:, 2, :, :], stat[:, 1, :, :], ACT.Sqrt).then_inc(rms_ready, 1)

        def source_hi(s):
            for t in range(TT):
                for half in range(2):
                    u = 2 * TT * s + 2 * t + half
                    act.wait_ge(src_transposed, u + 1)
                    nc.scalar.copy(s_hi[:, 4 * half:4 * half + 4, t * P:(t + 1) * P],
                                   ps[:, 5 + u % 3, :].rearrange("p (k c) -> p k c", k=4)).then_inc(shi_ready, 1)

        act.wait_ge(x_padded, 1)
        for t in range(TT):
            act.wait_ge(x_in[t], 16)
            if t:
                act.wait_ge(x_squared, t)
            nc.scalar.activation(psf[:, 0:D_MODEL], x_tok[:, t, :], ACT.Square,
                                 accum_out=stat[:, 0, t, 0:1]).then_inc(x_squared, 1)
        root()
        split_hi(act, 0, 0, 0 - PASS0)
        split_hi(act, 0, 0, 1 - PASS0)
        source_hi(0)
        split_hi(act, 0, 0, 2 - PASS0)

        for c, (kind, _, _) in enumerate(SECTION):
            split_hi(act, 0, 0, 2 * c + 3 - PASS0)
            if c >= 3:
                act.wait_ge(stage_stored[c % 3], stored(c - 3, c % 3))
            func = {"rg": ACT.Silu, "gr": ACT.Sigmoid, "gd": ACT.Sigmoid}.get(kind, ACT.Copy)
            for t in range(TT):
                u = TT * c + t
                wait_product(act, z_ready, 0, c, t)
                nc.scalar.activation(stage[:, c % 3, t, :], ps[:, u % 8, :], func).then_inc(z_evacuated, 1)
            if 2 * c + 4 < N0:
                split_hi(act, 0, 0, 2 * c + 4 - PASS0)
            if kind in ("k", "q"):
                root()

        act.wait_ge(lam_dots, 1)
        nc.scalar.activation(lam[:, 2:4], lam[:, 0:2], ACT.Exp).then_inc(lam_exps, 1)

        uses = [0]

        def evacuate(pairs):
            act.wait_ge(tr_ready, uses[0] + 1)
            for n, (dst, src) in enumerate(pairs):
                ins = nc.scalar.copy(dst, src)
                if n == len(pairs) - 1:
                    ins.then_inc(tr_evacuated, 1)
                else:
                    ins.then_inc(act_step, 1)
                    own.n += 1
            uses[0] += 1

        for g in range(UNITS + 2):
            if g < UNITS and g % TT == 0:
                hb = (g // TT) % 2
                for m in range(2):
                    for dst in (kT[:, hb, m, 0:PROMPT], kT[:, hb, m, PROMPT:PROMPT + PAST], qT[:, hb, m, 0:PROMPT]):
                        evacuate([(dst, ps[:, 4 + uses[0] % 2, :])])
                bank = ps[:, 4 + uses[0] % 2, :]
                evacuate([(kT[:, hb, :, PROMPT + PAST:KEYS], bank[:, 0:2 * SAMPLE].rearrange("p (m c) -> p m c", m=2)),
                          (qT[:, hb, :, PROMPT:ROWS], bank[:, P:3 * P].rearrange("p (m c) -> p m c", m=2))])
            if g < UNITS:
                act.wait_ge(max_ready, g + 1)
                width = unit_width(g % TT)
                for m in range(2):
                    nc.scalar.activation(prob[:, g % 2, m, 0:width], scores_view(g)[:, m, :], ACT.Exp,
                                         bias=neg_max[:, g, m:m + 1], scale=SC,
                                         accum_out=sums[:, g, m:m + 1]).then_inc(exp_ready, 1)
            if 1 <= g <= UNITS:
                u = g - 1
                n = min(u % TT + 1, PT)
                evacuate([(aT[:, u % 2, 0:n, :], ps[:, 4 + uses[0] % 2, 0:n * P].rearrange("p (k c) -> p k c", k=n))])
                if u % TT == PT:
                    evacuate([(aT[0:SAMPLE, u % 2, PT, :], ps[0:SAMPLE, 4 + uses[0] % 2, 0:P])])
            if g >= 2:
                u = g - 2
                act.wait_ge(o_copied, u + 1)
                if u:
                    act.wait_ge(o_squared, u)
                nc.scalar.activation(sq_att[:, :], od[:, u % TT, u // TT * DV:(u // TT + 1) * DV], ACT.Square,
                                     accum_out=stat[:, 0, u % TT, u // TT:u // TT + 1]).then_inc(o_squared, 1)
        root()

        for h in range(H):
            if h:
                act.wait_ge(qint_ready, h)
            for k, (dst, cols) in enumerate(((rqT[:, 0:PROMPT], PROMPT), (rkT[:, 0:PROMPT], PROMPT))):
                act.wait_ge(rtr_ready, 3 * h + k + 1)
                nc.scalar.copy(dst, ps[:, (3 * h + k) % 2, 0:cols]).then_inc(rtr_evacuated, 1)
            act.wait_ge(rtr_ready, 3 * h + 3)
            last = ps[:, (3 * h + 2) % 2, :]
            own.n += 1
            nc.scalar.copy(rqT[:, PROMPT:ROWS], last[:, 0:P]).then_inc(act_step, 1)
            nc.scalar.copy(rkT[:, PROMPT:ROWS], last[:, P:2 * P]).then_inc(rtr_evacuated, 1)
            for t in range(TT):
                u = TT * h + t
                act.wait_ge(ro_copied, u + 1)
                if u:
                    act.wait_ge(ro_squared, u)
                nc.scalar.activation(sq_ret[:, :], ro[:, t, h * DV:(h + 1) * DV], ACT.Square,
                                     accum_out=stat[:, 4, t, h:h + 1]).then_inc(ro_squared, 1)

        for p in range(3):
            if p == 0:
                source_hi(1)
                root()
            else:
                source_hi(1 + p)
            for c in (IN_CHUNKS + 2 * p, IN_CHUNKS + 2 * p + 1):
                for n in (2 * c + 3, 2 * c + 4):
                    if n < N0:
                        split_hi(act, 0, 0, n - PASS0)

        for t in range(TT):
            act.wait_ge(p_evacuated, TT * (OUT_CHUNKS - 1) + t + 1)
            act.wait_ge(x_squared, TT + t)
            nc.scalar.activation(psf[:, 5 * COLS:7 * COLS], x2[:, t, :], ACT.Square,
                                 accum_out=stat[:, 0, t, 0:1]).then_inc(x_squared, 1)
        root()
        for u in range(2 * TT):
            t, half = divmod(u, 2)
            act.wait_ge(h2_tr, u + 1)
            nc.scalar.copy(h2T[:, 4 * half:4 * half + 4, t * P:(t + 1) * P],
                           ps[:, 4 + u % 2, :].rearrange("p (k c) -> p k c", k=4)).then_inc(h2_evac, 1)

        for k in range(2):
            act.wait_ge(route_dve, k + 1)
            nc.scalar.activation(r4[:, 2 * k + 1], r4[:, 2 * k], ACT.Exp).then_inc(route_act, 1)

        def x_parts(i, e):
            for half in range(2):
                act.wait_ge(x_tr, 2 * e + half + 1)
                nc.scalar.copy(x_hi[:, 4 * half:4 * half + 4, :],
                               ps[:, 5 + half, :].rearrange("p (k c) -> p k c", k=4)).then_inc(xhi_ready, 1)

        def gate_silu(j, i, e):
            act.wait_ge(blocks_used, number(j, i, 4 if not isinstance(i, int) or i > 0 else 6))
            nc.scalar.activation(silu[:, :], ps[:, 0, :], ACT.Silu).then_inc(silu_ready, 1)

        def act_hi(e):
            act.wait_ge(a_tr, e + 1)
            nc.scalar.copy(a_hi[:, :, :], ps[:, 4, :].rearrange("p (k c) -> p k c", k=FK)).then_inc(ahi_ready, 1)

        def weigh(j, step, q_end, e):
            act.wait_ge(blocks_used, number(j, step, q_end))
            act.wait_ge(cur_ready, e + 1)
            for c in range(2):
                nc.scalar.activation(y_exp[:, c * COLS:(c + 1) * COLS], ps[:, 2 + c, :], ACT.Copy,
                                     scale=w_cur[:, 0:1]).then_inc(y_evac, 1)

        def step(j, i, last=False):
            e = NE * j + i
            act_hi(e - 1)
            for q in (6, 7) if last else (6, 7, 8):
                split_hi(act, j, i, q)
            gate_silu(j, i, e)
            if not last:
                x_parts(i + 1, e + 1)
                for q in (9, 10, 11):
                    split_hi(act, j, i, q)
            weigh(j, i, 6, e - 1)

        def expert_pass(j):
            for q in range(2, 8):
                split_hi(act, j, 0, q)
            x_parts(0, NE * j)
            for q in (8, 9, 10):
                split_hi(act, j, 0, q)
            gate_silu(j, 0, NE * j)
            x_parts(1, NE * j + 1)
            split_hi(act, j, 0, 11)
            with act.Fori(1, NE - 1) as i:
                step(j, i)
            step(j, NE - 1, last=True)
            act_hi(NE * j + NE - 1)
            weigh(j, NE, 2, NE * j + NE - 1)

        act.wait_ge(logits_ready, TT)
        act.wait_ge(y_init, 32)
        expert_pass(0)
        act.wait_ge(npass_ready, 1)
        passes = act.value_load(npass[0:1, 0:1], min_val=1, max_val=TT)
        with act.If(passes > 1):
            with act.Fori(1, passes) as j:
                expert_pass(j)

    @block.vector
    def _(dve):
        own = Steps(dve, dve_step)
        v = nc.vector
        roots = [0]

        def ask_root(src, count):
            roots[0] += 1
            v.tensor_scalar(stat[:, 1, :, :], src, 1.0 / count, EPS, ALU.mult, ALU.add).then_inc(ms_ready, 1)

        def take_root():
            dve.wait_ge(rms_ready, roots[0])
            own(v.reciprocal(stat[:, 3, :, :], stat[:, 2, :, :]))

        def source_lo(s, t):
            for half in range(2):
                u = 2 * TT * s + 2 * t + half
                dve.wait_ge(shi_ready, u + 1)
                part = slice(4 * half, 4 * half + 4), slice(t * P, (t + 1) * P)
                v.tensor_tensor(s_lo[:, part[0], part[1]], ps[:, 5 + u % 3, :].rearrange("p (k c) -> p k c", k=4),
                                s_hi[:, part[0], part[1]].bitcast(f32), ALU.subtract).then_inc(slo_ready, 1)

        own(v.memset(stat[:, :, :, :], 1.0))
        v.memset(x_tok[SAMPLE:P, PT, :], 0.0).then_inc(x_padded, 1)

        dve.wait_ge(x_squared, TT)
        ask_root(stat[:, 0, :, :], D_MODEL)
        take_root()
        dve.wait_ge(consts_in, 32)
        for t in range(TT + 1):
            if t < TT:
                if t >= 2:
                    dve.wait_ge(src_transposed, 2 * (t - 1))
                v.scalar_tensor_tensor(h_tok[:, t % 2, :], x_tok[:, t, :], stat[:, 3, t, 0:1], gmix[:, :],
                                       ALU.mult, ALU.mult).then_inc(src_ready, 1)
            if t >= 1:
                source_lo(0, t - 1)
            if t < 2:
                split_lo(dve, 0, 0, t - PASS0)
        dve.wait_ge(src_ready, TT)
        split_lo(dve, 0, 0, 2 - PASS0)
        dve.wait_ge(rot_in, 16 * 7)

        for c, (kind, _, _) in enumerate(SECTION):
            split_lo(dve, 0, 0, 2 * c + 3 - PASS0)
            zc = stage[:, c % 3, :, :]
            heads = zc.rearrange("p t (h c) -> p (t h) c", h=4)
            if c in DVE_CHUNKS[1:]:
                dve.wait_ge(z_staged, DVE_CHUNKS.index(c))
            if kind in ("k", "q"):
                for t in range(TT):
                    dve.wait_ge(z_evacuated, TT * c + t + 1)
                    own(v.tensor_tensor(sq_tmp[:, :], zc[:, t, :], zc[:, t, :], ALU.mult))
                    own(v.tensor_reduce(stat[:, 0, t, :], sq_tmp[:, :].rearrange("p (h c) -> p h c", h=4),
                                        AX.X, ALU.add))
                ask_root(stat[:, 0, :, :], DK)
            if kind in ("rq", "rk"):
                tab = 0 if kind == "rq" else 2
                for t in range(TT):
                    dve.wait_ge(z_evacuated, TT * c + t + 1)
                    zt = zc[:, t, :].rearrange("p (h c) -> p h c", h=4)
                    x_a, x_b = zt[:, :, 0:DK // 2], zt[:, :, DK // 2:DK]
                    cos, sin = (rot[:, tab + k, t:t + 1, :].to_broadcast([P, H, DK // 2]) for k in range(2))
                    v.tensor_tensor(rot_tmp[:, 0], x_a, cos, ALU.mult).then_inc(dve_step, 1)
                    v.tensor_tensor(rot_tmp[:, 1], x_b, sin, ALU.mult).then_inc(dve_step, 1)
                    v.tensor_tensor(rot_tmp[:, 2], x_a, sin, ALU.mult).then_inc(dve_step, 1)
                    own.n += 3
                    own(v.tensor_tensor(rot_tmp[:, 3], x_b, cos, ALU.mult))
                    v.tensor_tensor(x_a, rot_tmp[:, 0], rot_tmp[:, 1], ALU.subtract).then_inc(dve_step, 1)
                    own.n += 1
                    last = v.tensor_tensor(x_b, rot_tmp[:, 2], rot_tmp[:, 3], ALU.add)
                    if t < TT - 1:
                        own(last)
                    else:
                        last.then_inc(z_staged, 1)
            if 2 * c + 4 < N0:
                split_lo(dve, 0, 0, 2 * c + 4 - PASS0)
            if kind in ("k", "q"):
                gain = gk if kind == "k" else gq
                take_root()
                rstd = stat[:, 3, :, :].rearrange("p t (h o) -> p (t h) o", o=1).to_broadcast([P, TT * H, DK])
                own(v.tensor_tensor(heads, heads, rstd, ALU.mult))
                v.tensor_tensor(heads, heads, gain[:, :].unsqueeze(1).to_broadcast([P, TT * H, DK]),
                                ALU.mult).then_inc(z_staged, 1)

        dve.wait_ge(lam_loaded, 80)
        own(v.tensor_tensor(lam_in[:, 0::2, :], lam_in[:, 0::2, :], lam_in[:, 1::2, :], ALU.mult))
        v.tensor_reduce(lam[:, 0:2], lam_in[:, 0::2, :], AX.X, ALU.add).then_inc(lam_dots, 1)
        dve.wait_ge(lam_exps, 1)
        own(v.tensor_tensor(lam[:, 0:1], lam[:, 2:3], lam[:, 3:4], ALU.subtract))
        own(v.tensor_scalar(lam[:, 1:2], lam[:, 0:1], LAM_INIT, None, ALU.add))

        for g in range(UNITS + 2):
            if g < UNITS:
                dve.wait_ge(scores_ready, g + 1)
                own(v.tensor_reduce(neg_max[:, g, :], scores_view(g), AX.X, ALU.max))
                v.tensor_scalar(neg_max[:, g, :], neg_max[:, g, :], -SC, None, ALU.mult).then_inc(max_ready, 1)
            if 1 <= g <= UNITS:
                u = g - 1
                width = unit_width(u % TT)
                dve.wait_ge(exp_ready, 2 * (u + 1))
                p1, p2 = prob[:, u % 2, 0, 0:width], prob[:, u % 2, 1, 0:width]
                own(v.reciprocal(coef[:, u, :], sums[:, u, :]))
                own(v.tensor_tensor(coef[:, u, 1:2], coef[:, u, 1:2], lam[:, 1:2], ALU.mult))
                own(v.tensor_scalar(p2, p2, coef[:, u, 1:2], None, ALU.mult))
                v.scalar_tensor_tensor(p1, p1, coef[:, u, 0:1], p2, ALU.mult, ALU.subtract).then_inc(mix_ready, 1)
            if g >= 2:
                u = g - 2
                h, t = divmod(u, TT)
                dve.wait_ge(av_ready, u + 1)
                v.tensor_copy(od[:, t, h * DV:(h + 1) * DV], ps[:, 6 + u % 2, 0:DV]).then_inc(o_copied, 1)
        dve.wait_ge(o_squared, UNITS)
        ask_root(stat[:, 0, :, :], DV)
        take_root()
        own(v.tensor_scalar(stat[:, 3, :, :], stat[:, 3, :, :], 1.0 - LAM_INIT, None, ALU.mult))

        dve.wait_ge(ret_in, 48)
        for h in range(H):
            dve.wait_ge(ret_head_in[h % 2], 64 * (h // 2 + 1))
            v.tensor_tensor(kw[:, :, :], rk_tok[:, h % 2, :, :], wk[:, :, h:h + 1].to_broadcast([P, TT, DK]),
                            ALU.mult).then_inc(kw_ready, 1)
            dve.wait_ge(rtr_evacuated, 3 * (h + 1))
            v.tensor_tensor(q_int[:, :], rqT[:, PROMPT:ROWS], inter[:, h, :], ALU.mult).then_inc(qint_ready, 1)
            for m in range(TT):
                rows, width = (P, PROMPT - m * P) if m < PT else (SAMPLE, P)
                u = TT * h + m
                dve.wait_ge(s_ready, u + 1)
                v.tensor_tensor(sT[0:rows, ST_OFF[m]:ST_OFF[m] + width], ps[0:rows, 2 + u % 2, 0:width],
                                decay[0:rows, h, 0:width], ALU.mult).then_inc(s_decayed, 1)
            for t in range(TT):
                u = TT * h + t
                dve.wait_ge(ro_ready, u + 1)
                v.tensor_copy(ro[:, t, h * DV:(h + 1) * DV], ps[:, 4 + u % 2, 0:DV]).then_inc(ro_copied, 1)
            if h:
                dve.wait_ge(state_stored, 32 * h)
            dve.wait_ge(state_ready, 2 * h + 1)
            v.tensor_copy(st_out[:, 0, :], ps[:, 6, 0:DV]).then_inc(state_evacuated, 1)
            dve.wait_ge(state_ready, 2 * h + 2)
            v.scalar_tensor_tensor(st_out[:, 1, :], st_in[:, h % 2, :], GAMMA[h] ** SAMPLE, ps[:, 7, 0:DV],
                                   ALU.mult, ALU.add).then_inc(state_evacuated, 1)

        def head_norm(dst, t, gain):
            for h in range(H):
                part = dst[:, t, h * DV:(h + 1) * DV]
                ins = v.scalar_tensor_tensor(part, part, stat[:, 3, t, h:h + 1], gain[:, :], ALU.mult, ALU.mult)
                yield ins

        dve.wait_ge(o_copied, UNITS)
        for t in range(TT + 1):
            if t < TT:
                for h, ins in enumerate(head_norm(od, t, gsub)):
                    if h < H - 1:
                        own.n += 1
                        ins.then_inc(dve_step, 1)
                    else:
                        ins.then_inc(src_ready, 1)
            if t >= 1:
                source_lo(1, t - 1)
        dve.wait_ge(ro_squared, UNITS)
        dve.wait_ge(ro_copied, UNITS)
        ask_root(stat[:, 4, :, :], DV)
        take_root()
        for t in range(TT):
            for ins in head_norm(ro, t, gret):
                own(ins)
            for c in range(2):
                dve.wait_ge(gate_in[c], 16)
                part = ro[:, t, c * COLS:(c + 1) * COLS]
                ins = v.tensor_tensor(part, part, gate[:, c, t, :], ALU.mult)
                ins.then_inc(*((dve_step, 1) if c == 0 else (src_ready, 1)))
            own.n += 1

        def gate_value(n):
            return 16 * (n // 2 + 1) if n < 6 else 80

        for p in range(3):
            if p:
                for t in range(TT):
                    source_lo(1 + p, t)
            for j in range(2):
                c = IN_CHUNKS + 2 * p + j
                if 2 * c + 3 < N0:
                    split_lo(dve, 0, 0, 2 * c + 3 - PASS0)
                slot = j
                dve.wait_ge(gate_in[slot], gate_value(2 + 2 * p + j))
                for t in range(TT):
                    wait_product(dve, p_ready, IN_CHUNKS, c, t)
                    g_t, cols = gate[:, slot, t, :], slice(j * COLS, (j + 1) * COLS)
                    if p == 0:
                        v.tensor_tensor(md[:, t, cols], ps[:, t, :], g_t, ALU.mult).then_inc(p_evacuated, 1)
                    elif p == 1:
                        own(v.tensor_tensor(g_t, ps[:, t, :], g_t, ALU.mult))
                        v.tensor_tensor(md[:, t, cols], md[:, t, cols], g_t, ALU.add).then_inc(p_evacuated, 1)
                    else:
                        v.tensor_tensor(x2[:, t, cols], ps[:, t, :], g_t, ALU.add).then_inc(p_evacuated, 1)
                if 2 * c + 4 < N0:
                    split_lo(dve, 0, 0, 2 * c + 4 - PASS0)

        v.memset(zero_rows[:, :], 0.0).then_inc(zero_ready, 1)
        dve.wait_ge(x_squared, 2 * TT)
        ask_root(stat[:, 0, :, :], D_MODEL)
        take_root()
        dve.wait_ge(router_in, 48)
        for t in range(TT):
            v.scalar_tensor_tensor(h2[:, t, :], x2[:, t, :], stat[:, 3, t, 0:1], gffn[:, :],
                                   ALU.mult, ALU.mult).then_inc(h2_ready, 1)

        dve.wait_ge(logits_ready, TT)
        own(v.tensor_tensor(logit[:, :, :], ps[:, 7, 0:TT * (NG + NE)].rearrange("p (t c) -> p t c", t=TT),
                            r_bias[:, :].unsqueeze(1).to_broadcast([P, TT, NG + NE]), ALU.add))
        g_log = logit[:, :, 0:NG]
        e_log = logit[:, :, NG:NG + NE].rearrange("p t (g e) -> p t g e", g=NG)

        def wide(ap):
            return ap.to_broadcast([P, TT, 4])

        def first_of(mask, values, top, seen):
            own(v.tensor_tensor(mask, values, wide(top), ALU.is_equal))
            own(v.tensor_copy(seen, mask[:, :, 0:1]))
            for k in range(1, 4):
                own(v.tensor_tensor(mask[:, :, k:k + 1], mask[:, :, k:k + 1], seen, ALU.is_gt))
                own(v.tensor_tensor(seen, mask[:, :, k:k + 1], seen, ALU.max))

        own(v.tensor_reduce(r1[:, 0], g_log, AX.X, ALU.max))
        v.tensor_tensor(r4[:, 0], g_log, wide(r1[:, 0]), ALU.subtract).then_inc(route_dve, 1)
        g_mask = r4[:, 4]
        first_of(g_mask, g_log, r1[:, 0], r1[:, 1])
        prod4 = prod.rearrange("p t (g e) -> p t g e", g=NG)
        for t in range(TT):
            own(v.tensor_tensor(prod4[:, t], e_log[:, t], g_mask[:, t, :].unsqueeze(2).to_broadcast([P, NG, EPG]),
                                ALU.mult))
        own(v.tensor_reduce(r4[:, 5], prod.rearrange("p t (g e) -> p t e g", g=NG), AX.X, ALU.add))
        own(v.tensor_reduce(r1[:, 2], r4[:, 5], AX.X, ALU.max))
        v.tensor_tensor(r4[:, 2], r4[:, 5], wide(r1[:, 2]), ALU.subtract).then_inc(route_dve, 1)
        dve.wait_ge(route_act, 1)
        own(v.tensor_reduce(r1[:, 3], r4[:, 1], AX.X, ALU.add))
        own(v.reciprocal(r1[:, 4], r1[:, 3]))
        dve.wait_ge(route_act, 2)
        e_p, first, second = r4[:, 3], r4[:, 6], r4[:, 7]
        own(v.tensor_reduce(r1[:, 5], e_p, AX.X, ALU.max))
        first_of(first, e_p, r1[:, 5], r1[:, 6])
        own(v.scalar_tensor_tensor(r4[:, 8], first, -2.0, e_p, ALU.mult, ALU.add))
        own(v.tensor_reduce(r1[:, 7], r4[:, 8], AX.X, ALU.max))
        first_of(second, r4[:, 8], r1[:, 7], r1[:, 8])
        own(v.tensor_tensor(r1[:, 9], r1[:, 5], r1[:, 7], ALU.add))
        own(v.reciprocal(r1[:, 10], r1[:, 9]))
        own(v.tensor_tensor(r1[:, 10], r1[:, 10], r1[:, 4], ALU.mult))
        own(v.tensor_tensor(r4[:, 9], first, second, ALU.add))
        own(v.tensor_tensor(r4[:, 8], e_p, r4[:, 9], ALU.mult))
        own(v.tensor_tensor(r4[:, 8], r4[:, 8], wide(r1[:, 10]), ALU.mult))
        own(v.tensor_tensor(r4[:, 9], r4[:, 9], wide(tok_valid.unsqueeze(2)), ALU.mult))
        sel4, wt4 = (x.rearrange("p t (g e) -> p t g e", g=NG) for x in (sel, wt))
        for t in range(TT):
            groups = g_mask[:, t, :].unsqueeze(2).to_broadcast([P, NG, EPG])
            own(v.tensor_tensor(wt4[:, t], groups, r4[:, 8, t:t + 1, :].to_broadcast([P, NG, EPG]), ALU.mult))
            ins = v.tensor_tensor(sel4[:, t], groups, r4[:, 9, t:t + 1, :].to_broadcast([P, NG, EPG]), ALU.mult)
            if t < TT - 1:
                own(ins)
            else:
                ins.then_inc(sel_ready, 1)
        own(v.tensor_copy(slot_rhs[:, :, :, 0], tok_plus1.unsqueeze(2).to_broadcast([P, TT, NE])))
        own(v.tensor_copy(slot_rhs[:, :, :, 1], wt))
        dve.wait_ge(sel_ready, 1)
        own(v.tensor_scalar(prod, sel, -1e6, 1e6, ALU.mult, ALU.add))
        dve.wait_ge(pos_ready, 1)
        own(v.tensor_tensor(posm, prod, ps[:, 6, 0:TT * NE].rearrange("p (t e) -> p t e", t=TT), ALU.add))
        own(v.tensor_reduce(cmax[:, 0:1], ps[:, 6, TT * NE:(TT + 1) * NE], AX.X, ALU.max))
        for k in range(1, TT):
            own(v.tensor_scalar(cmax[:, k:k + 1], cmax[:, 0:1], float(P * k), None, ALU.is_gt))
        own(v.tensor_reduce(cmax[:, 5:6], cmax[:, 1:TT], AX.X, ALU.add))
        v.tensor_scalar(npass[0:1, 0:1], cmax[0:1, 5:6], 1.0, None, ALU.add).then_inc(npass_ready, 1)

        LIST_STEPS = 4

        def lists(j):
            if not isinstance(j, int):
                dve.wait_ge(y_scattered, 16 * NE * j)
                own(v.tensor_scalar(posm, posm, -float(P), None, ALU.add))
            for e in range(NE):
                if e >= 2:
                    dve.wait_ge(onehot_used, NE * j + e - 1)
                v.tensor_tensor(onehot[:, e % 2, :, :], iota.unsqueeze(1).to_broadcast([P, TT, P]),
                                posm[:, :, e:e + 1].to_broadcast([P, TT, P]), ALU.is_equal).then_inc(onehot_ready, 1)
            dve.wait_ge(onehot_used, NE * j + NE)
            got = ps[:, 7, 0:2 * NE].rearrange("p (e k) -> p e k", k=2)
            own(v.tensor_scalar(slot_tmp[:, 0, :], got[:, :, 0], 0.0, None, ALU.is_equal))
            own(v.scalar_tensor_tensor(slot_tmp[:, 1, :], slot_tmp[:, 0, :], sink_plus1, got[:, :, 0],
                                       ALU.mult, ALU.add))
            own(v.tensor_scalar(s_idx[:, :], slot_tmp[:, 1, :], -1.0, None, ALU.add))
            own(v.tensor_scalar(g_idx[:, :], got[:, :, 0], -1.0, 0.0, ALU.add, ALU.max))
            v.tensor_copy(slot_w[:, :], got[:, :, 1]).then_inc(lists_ready, 1)

        def x_parts(e):
            for half in range(2):
                dve.wait_ge(xhi_ready, 2 * e + half + 1)
                part = slice(4 * half, 4 * half + 4)
                v.tensor_tensor(x_lo[:, part, :], ps[:, 5 + half, :].rearrange("p (k c) -> p k c", k=4),
                                x_hi[:, part, :].bitcast(f32), ALU.subtract).then_inc(xlo_ready, 1)

        def gated(e):
            dve.wait_ge(silu_ready, e + 1)
            v.tensor_tensor(act_t[:, :], ps[:, 1, :], silu[:, :], ALU.mult).then_inc(act_ready, 1)

        def act_lo(e):
            dve.wait_ge(ahi_ready, e + 1)
            v.tensor_tensor(a_lo[:, :, :], ps[:, 4, :].rearrange("p (k c) -> p k c", k=FK),
                            a_hi[:, :, :].bitcast(f32), ALU.subtract).then_inc(alo_ready, 1)

        def step(j, i, last=False):
            e = NE * j + i
            act_lo(e - 1)
            for q in (6, 7) if last else (6, 7, 8):
                split_lo(dve, j, i, q)
            gated(e)
            if not last:
                x_parts(e + 1)
                for q in (9, 10, 11):
                    split_lo(dve, j, i, q)

        before = own.n

        def expert_pass(j):
            if not isinstance(j, int):
                own.base, own.n = (LIST_STEPS + 1) * (j - 1), before + LIST_STEPS
            lists(j)
            if isinstance(j, int):
                dve.wait_ge(y_init, 32)
                dve.wait_ge(h2_stored, 16)
            for q in range(2, 8):
                split_lo(dve, j, 0, q)
            x_parts(NE * j)
            for q in (8, 9, 10):
                split_lo(dve, j, 0, q)
            gated(NE * j)
            x_parts(NE * j + 1)
            split_lo(dve, j, 0, 11)
            with dve.Fori(1, NE - 1) as i:
                step(j, i)
            step(j, NE - 1, last=True)
            act_lo(NE * j + NE - 1)

        expert_pass(0)
        assert own.n == before + LIST_STEPS
        passes = dve.value_load(npass[0:1, 0:1], min_val=1, max_val=TT)
        with dve.If(passes > 1):
            with dve.Fori(1, passes) as j:
                expert_pass(j)

    @block.tensor
    def _(pe):
        mm, transpose = nc.tensor.matmul, nc.tensor.transpose

        def source(s, src, ready):
            for t in range(TT):
                ready(t)
                for half in range(2):
                    u = 2 * TT * s + 2 * t + half
                    if u >= 3:
                        pe.wait_ge(slo_ready, u - 2)
                    for k in range(4):
                        col = (4 * half + k) * P
                        last = transpose(ps[:, 5 + u % 3, k * P:(k + 1) * P], src(t)[:, col:col + P], ident)
                    last.then_inc(src_transposed, 1)

        def chunk(c, banks, free, ready):
            for half in range(BPC):
                n = 2 * c + half
                q = n - PASS0
                pe.wait_ge(lo_ready, n + 1)
                for kk in range(4):
                    k = 4 * half + kk
                    cols = slice(kk * COLS, (kk + 1) * COLS)
                    for t in range(TT):
                        if k == 0:
                            free(t)
                        rows = slice(t * P, (t + 1) * P)
                        last = product(banks(t), s_hi[:, k, rows], s_lo[:, k, rows], w_hi[:, q % SPL, cols],
                                       w_lo[:, q % SPL, cols], k == 0, k == KC - 1)
                        if k == KC - 1 and t < TT - 1:
                            last.then_inc(ready, 1)
                last.then_inc(blocks_used, 1)

        pe.wait_ge(consts_in, 32)
        source(0, lambda t: h_tok[:, t % 2, :], lambda t: pe.wait_ge(src_ready, t + 1))
        pe.wait_ge(slo_ready, 2 * TT)

        def in_free(c, t):
            if TT * c + t >= 8:
                pe.wait_ge(z_evacuated, TT * c + t - 7)

        for c in range(IN_CHUNKS):
            chunk(c, lambda t: ps[:, (TT * c + t) % 8, :], lambda t: in_free(c, t), z_ready)

        pe.wait_ge(z_evacuated, TT * IN_CHUNKS)
        pe.wait_ge(lam_loaded, 80)
        uses = [0]

        def transposes(parts):
            if uses[0] >= 2:
                pe.wait_ge(tr_evacuated, uses[0] - 1)
            bank = ps[:, 4 + uses[0] % 2, :]
            for out, src in parts:
                rows = src.shape[0]
                last = transpose(out(bank), src, ident[0:rows, 0:rows])
            last.then_inc(tr_ready, 1)
            uses[0] += 1

        def four(tile_of):
            return [(lambda bank, t=t: bank[:, t * P:(t + 1) * P], tile_of(t)) for t in range(PT)]

        for g in range(UNITS + 2):
            h, t = divmod(g, TT)
            if g < UNITS and t == 0:
                pe.wait_ge(kq_in, 64 * (h + 1))
                for m in range(2):
                    cols = slice(m * DK, (m + 1) * DK)
                    transposes(four(lambda t: k_tok[:, t, cols]))
                    transposes(four(lambda t: kc_tok[:, t, cols]))
                    transposes(four(lambda t: q_tok[:, t, cols]))
                transposes([(lambda b, m=m: b[:, m * SAMPLE:(m + 1) * SAMPLE],
                             k_tok[0:SAMPLE, PT, m * DK:(m + 1) * DK]) for m in range(2)] +
                           [(lambda b, m=m: b[:, (m + 1) * P:(m + 2) * P],
                             q_tok[:, PT, m * DK:(m + 1) * DK]) for m in range(2)])
                assert uses[0] == head_transposed(h)
                pe.wait_ge(tr_evacuated, head_transposed(h))
            if g < UNITS:
                if t == PT or (t == 0 and g):
                    pe.wait_ge(exp_ready, 2 * g)
                elif g >= 2:
                    pe.wait_ge(exp_ready, 2 * (g - 1))
                hb, width = h % 2, unit_width(t)
                for m in range(2):
                    q = qT[:, hb, m, t * P:(t + 1) * P]
                    if t < PT:
                        out = ps[:, 2 * (g % 2) + m, 0:width]
                        mm(out, q, kT[:, hb, m, 0:width], start=True, stop=False)
                        last = mm(out[:, width - P:width], hide[0:1, 0:P], hide[0:1, P:2 * P],
                                  start=False, stop=True)
                    else:
                        mm(psf[:, 2 * m * COLS:2 * m * COLS + PAST], q, kT[:, hb, m, PROMPT:PROMPT + PAST],
                           start=True, stop=True)
                        last = mm(psf[:, 2 * m * COLS + PAST:2 * m * COLS + PAST + SAMPLE], q,
                                  kT[:, hb, m, PROMPT + PAST:KEYS], start=True, stop=True)
                last.then_inc(scores_ready, 1)
            if 1 <= g <= UNITS:
                u = g - 1
                mixed = prob[:, u % 2, 0, :]
                pe.wait_ge(mix_ready, u + 1)
                n = min(u % TT + 1, PT)
                transposes(four(lambda k: mixed[:, k * P:(k + 1) * P])[0:n])
                if u % TT == PT:
                    transposes([(lambda b: b[0:SAMPLE, 0:P], mixed[:, PAST:PAST + SAMPLE])])
                assert uses[0] == unit_transposed(u)
            if g >= 2:
                u = g - 2
                uh, ut = divmod(u, TT)
                if ut == 0:
                    pe.wait_ge(v_in[uh % 2], 48 * (uh // 2 + 1))
                if u >= 2:
                    pe.wait_ge(o_copied, u - 1)
                pe.wait_ge(tr_evacuated, unit_transposed(u))
                out = ps[:, 6 + u % 2, 0:DV]
                if ut < PT:
                    for k in range(ut + 1):
                        last = mm(out, aT[:, u % 2, k, :], v_tok[:, uh % 2, k, :], start=k == 0, stop=k == ut)
                else:
                    for k in range(PT):
                        mm(out, aT[:, u % 2, k, :], vc_tok[:, uh % 2, k, :], start=k == 0, stop=False)
                    last = mm(out, aT[0:SAMPLE, u % 2, PT, :], v_tok[0:SAMPLE, uh % 2, PT, :],
                              start=False, stop=True)
                last.then_inc(av_ready, 1)

        for h in range(H):
            hb = h % 2
            pe.wait_ge(ret_head_in[hb], 64 * (h // 2 + 1))
            if h == 0:
                pe.wait_ge(exp_ready, 2 * UNITS)
            for k, parts in enumerate(([(rq_tok, t) for t in range(PT)], [(rk_tok, t) for t in range(PT)],
                                       [(rq_tok, PT), (rk_tok, PT)])):
                u = 3 * h + k
                if u >= 2:
                    pe.wait_ge(rtr_evacuated, u - 1)
                for n, (src, t) in enumerate(parts):
                    last = transpose(ps[:, u % 2, n * P:(n + 1) * P], src[:, hb, t, :], ident)
                last.then_inc(rtr_ready, 1)
            pe.wait_ge(rtr_evacuated, 3 * (h + 1))
            for m in range(TT):
                u = TT * h + m
                if u >= 2:
                    pe.wait_ge(s_decayed, u - 1)
                rows, width = (P, PROMPT - m * P) if m < PT else (SAMPLE, P)
                mm(ps[0:rows, 2 + u % 2, 0:width], rkT[:, m * P:m * P + rows], rqT[:, m * P:m * P + width],
                   start=True, stop=True).then_inc(s_ready, 1)
            for t in range(TT):
                u = TT * h + t
                if h == 0 and t == 0:
                    pe.wait_ge(tr_evacuated, unit_transposed(UNITS - 1))
                if u >= 2:
                    pe.wait_ge(ro_copied, u - 1)
                out = ps[:, 4 + u % 2, 0:DV]
                if t < PT:
                    pe.wait_ge(s_decayed, TT * h + t + 1)
                    for m in range(t + 1):
                        at_ = ST_OFF[m] + (t - m) * P
                        last = mm(out, sT[:, at_:at_ + P], rv_tok[:, hb, m, :], start=m == 0, stop=m == t)
                else:
                    pe.wait_ge(s_decayed, TT * (h + 1))
                    pe.wait_ge(qint_ready, h + 1)
                    mm(out, sT[0:SAMPLE, ST_OFF[PT]:ST_OFF[PT] + P], rv_tok[0:SAMPLE, hb, PT, :],
                       start=True, stop=False)
                    last = mm(out, q_int[:, :], st_in[:, hb, :], start=False, stop=True)
                last.then_inc(ro_ready, 1)
            pe.wait_ge(kw_ready, h + 1)
            if h == 0:
                pe.wait_ge(o_copied, UNITS)
            else:
                pe.wait_ge(state_evacuated, 2 * h)
            for t in range(PT):
                last = mm(ps[:, 6, 0:DV], kw[:, t, :], rv_tok[:, hb, t, :], start=t == 0, stop=t == PT - 1)
            last.then_inc(state_ready, 1)
            mm(ps[:, 7, 0:DV], kw[0:SAMPLE, PT, :], rv_tok[0:SAMPLE, hb, PT, :], start=True, stop=True)\
                .then_inc(state_ready, 1)

        pe.wait_ge(state_evacuated, 2 * H)
        pe.wait_ge(ro_copied, UNITS)

        def out_free(x, t):
            if x:
                pe.wait_ge(p_evacuated, TT * (x - 1) + t + 1)

        for p, src in enumerate((od, ro, md)):
            if p < 2:
                source(1 + p, lambda t: src[:, t, :], lambda t: pe.wait_ge(src_ready, TT * (1 + p) + t + 1))
            else:
                source(1 + p, lambda t: src[:, t, :], lambda t: pe.wait_ge(p_evacuated, TT * 3 + t + 1))
            pe.wait_ge(slo_ready, 2 * TT * (2 + p))
            for x in (2 * p, 2 * p + 1):
                chunk(IN_CHUNKS + x, lambda t: ps[:, t, :], lambda t: out_free(x, t), p_ready)

        pe.wait_ge(router_in, 48)
        for t in range(TT + 1):
            if t < TT:
                pe.wait_ge(h2_ready, t + 1)
                if t == 0:
                    pe.wait_ge(p_evacuated, TT * OUT_CHUNKS)
                for half in range(2):
                    u = 2 * t + half
                    if u >= 2:
                        pe.wait_ge(h2_evac, u - 1)
                    for k in range(4):
                        col = (4 * half + k) * P
                        last = transpose(ps[:, 4 + u % 2, k * P:(k + 1) * P], h2[:, t, col:col + P], ident)
                    last.then_inc(h2_tr, 1)
            if t >= 1:
                s = t - 1
                pe.wait_ge(h2_evac, 2 * (s + 1))
                for k in range(KC):
                    last = mm(ps[:, 7, s * (NG + NE):(s + 1) * (NG + NE)], h2T[:, k, s * P:(s + 1) * P],
                              w_r[:, k, :], start=k == 0, stop=k == KC - 1)
                last.then_inc(logits_ready, 1)
        pe.wait_ge(sel_ready, 1)
        for t in range(TT):
            for s in range(t + 1):
                mm(ps[:, 6, t * NE:(t + 1) * NE], tri if s == t else ones, sel[:, s, :], start=s == 0, stop=s == t)
        for s in range(TT):
            last = mm(ps[:, 6, TT * NE:(TT + 1) * NE], ones, sel[:, s, :], start=s == 0, stop=s == TT - 1)
        last.then_inc(pos_ready, 1)

        def lists(j):
            for e in range(NE):
                pe.wait_ge(onehot_ready, NE * j + e + 1)
                for t in range(TT):
                    last = mm(ps[:, 7, 2 * e:2 * e + 2], onehot[:, e % 2, t, :], slot_rhs[:, t, e, :],
                              start=t == 0, stop=t == TT - 1)
                last.then_inc(onehot_used, 1)

        def rows_in(e, first=False):
            pe.wait_ge(x_gathered, 16 * (e + 1))
            if not first:
                pe.wait_ge(xlo_ready, 2 * e)
            for half in range(2):
                for k in range(4):
                    col = (4 * half + k) * P
                    last = transpose(ps[:, 5 + half, k * P:(k + 1) * P], x_exp[:, col:col + P], ident)
                last.then_inc(x_tr, 1)

        def up_gate(j, i, e, q0, first=False):
            pe.wait_ge(xlo_ready, 2 * (e + 1))
            if not first:
                pe.wait_ge(act_ready, e)
            for b in range(4):
                q = q0 + b
                pe.wait_ge(lo_ready, number(j, i, q) + 1)
                for kk in range(4):
                    k, cols = 4 * (b % 2) + kk, slice(kk * COLS, (kk + 1) * COLS)
                    last = product(ps[:, 1 - b // 2, :], x_hi[:, k, :], x_lo[:, k, :], hi_of(q)[:, cols],
                                   lo_of(q)[:, cols], k == 0, k == KC - 1)
                last.then_inc(blocks_used, 1)

        def acts_in(e):
            pe.wait_ge(act_ready, e + 1)
            for k in range(FK):
                last = transpose(ps[:, 4, k * P:(k + 1) * P], act_t[:, k * P:(k + 1) * P], ident)
            last.then_inc(a_tr, 1)

        def down(j, i, e, q0, first=False):
            pe.wait_ge(alo_ready, e + 1)
            if not first:
                pe.wait_ge(y_evac, 2 * e)
            for b in range(2):
                q = q0 + b
                pe.wait_ge(lo_ready, number(j, i, q) + 1)
                for kk in range(2):
                    for c in range(2):
                        k, cols = 2 * b + kk, slice((2 * kk + c) * COLS, (2 * kk + c + 1) * COLS)
                        last = product(ps[:, 2 + c, :], a_hi[:, k, :], a_lo[:, k, :], hi_of(q)[:, cols],
                                       lo_of(q)[:, cols], k == 0, k == FK - 1)
                last.then_inc(blocks_used, 1)

        def expert_pass(j):
            e0 = NE * j
            first = isinstance(j, int)
            lists(j)
            rows_in(e0, first)
            up_gate(j, 0, e0, 2, first)
            rows_in(e0 + 1)
            acts_in(e0)
            up_gate(j, 1, e0 + 1, 0)
            rows_in(e0 + 2)
            down(j, 1, e0, 4, first)
            with pe.Fori(2, NE - 1) as i:
                acts_in(e0 + i - 1)
                up_gate(j, i, e0 + i, 0)
                rows_in(e0 + i + 1)
                down(j, i, e0 + i - 1, 4)
            acts_in(e0 + NE - 2)
            up_gate(j, NE - 1, e0 + NE - 1, 0)
            down(j, NE - 1, e0 + NE - 2, 4)
            acts_in(e0 + NE - 1)
            down(j, NE, e0 + NE - 1, 0)

        expert_pass(0)
        pe.wait_ge(npass_ready, 1)
        passes = pe.value_load(npass[0:1, 0:1], min_val=1, max_val=TT)
        with pe.If(passes > 1):
            with pe.Fori(1, passes) as j:
                expert_pass(j)

    block.__exit__(None, None, None)


def stored(c, s):
    return sum(32 if SECTION[k][0] in ("k", "v") else 16 for k in range(c + 1) if k % 3 == s)


_INS = ["x_prompt", "x_sample", "cache_k", "cache_v", "state_ret", "g_mix", "w_in", "g_q", "g_k", "lambda_q1",
        "lambda_k1", "lambda_q2", "lambda_k2", "g_ret", "w_ret_o", "g_sub", "w_diff_o", "w_out", "g_ffn", "w_group",
        "b_group", "w_expert", "b_expert", "w_gate", "w_up", "w_down"]
_OUTS = {"y": (SINK + P, D_MODEL), "k_new": (REAL, D_MODEL), "v_new": (REAL, D_MODEL),
         "s_prompt": (H, DK, DV), "s_sample": (H, DK, DV)}


def kernel(**inputs):
    import concourse.bacc as bacc
    from concourse.bass_utils import run_bass_kernel_spmd

    nc = bacc.Bacc("TRN2", target_bir_lowering=False, num_devices=1)
    arrays, ins = {}, {}
    for name, arr in [(n, inputs[n]) for n in _INS] + list(shape_constants().items()):
        arr = np.ascontiguousarray(arr)
        arrays[f"in_{name}"] = arr
        ins[name] = nc.dram_tensor(f"in_{name}", arr.shape, mybir.dt.from_np(arr.dtype), kind="ExternalInput").ap()
    outs = {n: nc.dram_tensor(f"out_{n}", s, mybir.dt.float32, kind="ExternalOutput").ap() for n, s in _OUTS.items()}
    build(nc, ins, outs)
    r = run_bass_kernel_spmd(nc, [arrays], core_ids=[0]).results[0]
    y, k, v, s_p, s_s = (r[f"out_{n}"] for n in _OUTS)
    return (y[None, :PROMPT], y[None, PROMPT:REAL],
            k[:PROMPT].reshape(1, 1, PROMPT, H, DV), v[:PROMPT].reshape(1, 1, PROMPT, H, DV), s_p[None, None],
            k[PROMPT:].reshape(1, 1, SAMPLE, H, DV), v[PROMPT:].reshape(1, 1, SAMPLE, H, DV), s_s[None, None])
```

```python
import math
import numpy as np
import concourse.bass as bass
from concourse import mybir

P = 128
D_MODEL = 1024
PROMPT = 512
SAMPLE = 64
PAST = 512
CHUNK = 64
TT = 5
PT = PROMPT // P
ROWS = TT * P
REAL = PROMPT + SAMPLE
EPS = 1e-6
H = 4
DK = 128
DV = 256
IN_W = 8192
KC = D_MODEL // P
COLS = 512
NE, NG, EPG = 16, 4, 4
NR = NG + NE
POOL_SPLITS = 4
SR = 5
D_FF = 512
FK = D_FF // P
BLK = 2048
RAW, SPL = 6, 3
IN_CHUNKS = IN_W // COLS
OUT_CHUNKS = 3 * D_MODEL // COLS
CHUNKS = IN_CHUNKS + OUT_CHUNKS
BPC = D_MODEL * COLS // P // BLK
N0 = CHUNKS * BPC
EB = 6
PASS_BLOCKS = EB * NE
UNITS = H * TT
KEYS = PROMPT + PAST + SAMPLE
SC = DK ** -0.5
NEG = -1e30
HEAD_USES = 7
LAM_INIT = 0.8 - 0.6 * math.exp(0.0)
SINK = ROWS

SECTION = [("k", 4096, 0), ("k", 4608, 512), ("q", 3072, 0), ("q", 3584, 512), ("v", 5120, 0), ("v", 5632, 512),
           ("rq", 0, 0), ("rk", 512, 0), ("rv", 1024, 0), ("rv", 1536, 512), ("rg", 2048, 0), ("rg", 2560, 512),
           ("gr", 6144, 0), ("gr", 6656, 512), ("gd", 7168, 0), ("gd", 7680, 512)]

DVE_CHUNKS = [c for c, (kind, _, _) in enumerate(SECTION) if kind in ("k", "q", "rq", "rk")]

GAMMA = [1.0 - 2.0 ** (-5.0 - h) for h in range(H)]


def shape_constants():
    f = np.float32
    p = np.arange(P)
    tok = np.arange(ROWS).reshape(TT, P).T
    gen = np.concatenate([np.eye(P), (p[:, None] < p[None, :]), np.ones((P, P)), np.tile(p, (P, 1)),
                          tok + 1, tok < REAL, (SINK + 1 + p)[:, None], np.tile([4, 3, 2, 1], (P, 1)),
                          np.tile(P * np.arange(TT), (P, 1))],
                         axis=1).astype(f)
    inv = (f(1.0) / (f(10000.0) ** np.linspace(0.0, 1.0, DK // 2, dtype=f))).astype(f)
    ang = (tok.astype(f)[:, :, None] * inv[None, None, :]).astype(f).astype(np.float64)
    rot = np.stack([np.cos(ang), np.sin(ang), np.cos(ang) * SC, np.sin(ang) * SC], axis=1).astype(f)
    dec = np.zeros((P, H, COLS))
    inter = np.zeros((P, H, P))
    wk = np.zeros((P, TT, H))
    m, n = p[:, None], np.arange(COLS)[None, :]
    seen = (m // CHUNK) <= (n // CHUNK)
    for h, g in enumerate(GAMMA):
        apart = np.where((m // CHUNK) == (n // CHUNK), np.abs(n - m), n - m)
        dec[:, h] = np.where(seen, g ** np.where(seen, apart, 0).astype(np.float64), 0.0)
        inter[:, h] = g ** (p[None, :] + 1.0)
        for t in range(PT):
            wk[:, t, h] = g ** (PROMPT - 1.0 - (t * P + p))
        wk[:SAMPLE, PT, h] = g ** (SAMPLE - 1.0 - p[:SAMPLE])
    ret = np.concatenate([dec.reshape(P, -1), inter.reshape(P, -1), wk.reshape(P, -1)], axis=1).astype(f)
    hide = np.concatenate([np.where(p < CHUNK, NEG, 0.0), np.where(p >= CHUNK, 1.0, 0.0)])[None, :].astype(f)
    return {"c_gen": gen, "c_rot": rot.reshape(P, -1), "c_ret": ret, "c_hide": hide}


class Steps:

    def __init__(self, eng, sem):
        self.eng, self.sem, self.n, self.base = eng, sem, 0, 0

    def __call__(self, ins):
        self.n += 1
        ins.then_inc(self.sem, 1)
        self.eng.wait_ge(self.sem, self.base + self.n)


def build(nc, a, o):
    f32, f32r, u32, i32 = mybir.dt.float32, mybir.dt.float32r, mybir.dt.uint32, mybir.dt.int32
    bf16 = mybir.dt.bfloat16
    ALU, ACT, AX = mybir.AluOpType, mybir.ActivationFunctionType, mybir.AxisListType

    end = [0]

    def at(name, shape, dt, offset):
        size = (2 if dt == mybir.dt.bfloat16 else 4) * int(np.prod(shape[1:]))
        end[0] = offset + (size + 31) // 32 * 32
        assert end[0] <= nc.sbuf_top, (name, end[0])
        return nc.alloc_sbuf_tensor_at(name, shape, dt, offset=offset)

    def after(name, shape, dt):
        return at(name, shape, dt, end[0])

    raw = at("raw", [P, RAW, BLK], f32, (nc.sbuf_base + 31) // 32 * 32)
    w_hi = after("w_hi", [P, SPL, BLK], f32r)
    w_lo = after("w_lo", [P, SPL, BLK], f32r)
    BIG = end[0]
    s_hi = after("s_hi", [P, KC, ROWS], f32r)
    s_lo = after("s_lo", [P, KC, ROWS], f32r)
    gen = after("gen", [P, 4 * P + 3 * TT + 5], f32)
    ident, tri, ones, iota = (gen[:, i * P:(i + 1) * P] for i in range(4))
    tok_plus1 = gen[:, 4 * P:4 * P + TT]
    tok_valid = gen[:, 4 * P + TT:4 * P + 2 * TT]
    sink_plus1 = gen[:, 4 * P + 2 * TT:4 * P + 2 * TT + 1]
    tile_row = gen[:, 4 * P + 2 * TT + 5:4 * P + 3 * TT + 5]
    earlier = gen[:, 4 * P + 2 * TT + 1:4 * P + 2 * TT + 5]
    gret, gsub = after("gret", [P, DV], f32), after("gsub", [P, DV], f32)
    GSUB = end[0] - 4 * DV
    gq, gk = after("gq", [P, DK], f32), after("gk", [P, DK], f32)
    w_rs = at("w_rs", [P, KC, 2 * NR], f32r, GSUB)
    w_r = after("w_r", [P, KC, NR], f32)
    assert end[0] <= GSUB + 4 * (DV + 2 * DK)
    end[0] = GSUB + 4 * (DV + 2 * DK)
    r_bias = after("r_bias", [P, NG + NE], f32)
    lam = after("lam", [P, 4], f32)
    x_rstd = after("x_rstd", [P, TT], f32)
    tri16, ones16 = after("tri16", [P, P], bf16), after("ones16", [P, P], bf16)
    stat = after("stat", [P, 5, TT, H], f32)
    REGION = end[0]
    rot = at("rot", [P, 4, TT, DK // 2], f32, REGION)
    stage = after("stage", [P, 3, TT, COLS], f32)
    X_TOK = end[0]
    x_tok = after("x_tok", [P, TT, D_MODEL], f32)
    h_tok = after("h_tok", [P, 2, D_MODEL], f32)
    sq_tmp = at("sq_tmp", [P, COLS], f32, end[0] - 8192)
    rot_tmp = at("rot_tmp", [P, 4, H, DK // 2], f32, end[0])
    gmix = at("gmix", [P, D_MODEL], f32, BIG - 4 * BLK)
    kT0, qT0 = at("kT0", [P, 2, KEYS], f32, BIG), after("qT0", [P, 2, ROWS], f32)
    EARLY = end[0] + 4096
    kT1, qT1 = at("kT1", [P, 2, KEYS], f32, EARLY), after("qT1", [P, 2, ROWS], f32)
    kT, qT = (kT0, kT1), (qT0, qT1)
    prob = after("prob", [P, 2, 2, PAST + SAMPLE], f32)
    assert end[0] <= BIG + 40960
    od = at("od", [P, TT, D_MODEL], f32, REGION)
    ro = after("ro", [P, TT, D_MODEL], f32)
    FREE = end[0]
    vc_tok = at("vc_tok", [P, 2, PT, DV], f32, REGION + 20480)
    aT = after("aT", [P, 2, TT, P], f32)
    sq_att = after("sq_att", [P, DV], f32)
    assert end[0] <= X_TOK
    k_tok = at("k_tok", [P, TT, DV], f32, X_TOK)
    kc_tok = after("kc_tok", [P, PT, DV], f32)
    q_tok = after("q_tok", [P, TT, DV], f32)
    V_TOK = end[0]
    v_tok = after("v_tok", [P, 2, TT, DV], f32)
    neg_max = after("neg_max", [P, UNITS, 2], f32)
    sums = after("sums", [P, UNITS, 2], f32)
    coef = after("coef", [P, UNITS, 2], f32)
    lam_in = after("lam_in", [P, 4, DK], f32)
    hide = after("hide", [1, 2 * P], f32)
    decay = at("decay", [P, H, COLS], f32, BIG)
    inter = after("inter", [P, H, P], f32)
    wk = after("wk", [P, TT, H], f32)
    rv_tok = after("rv_tok", [P, 2, TT, DV], f32)
    assert end[0] - TT * DV * 4 <= EARLY
    rqT = after("rqT", [P, ROWS], f32)
    rkT = after("rkT", [P, ROWS], f32)
    ST_OFF = [0, 512, 896, 1152, 1280]
    sT = after("sT", [P, 1280 + P], f32)
    q_int = after("q_int", [P, P], f32)
    kw = after("kw", [P, TT, DK], f32)
    sq_ret = after("sq_ret", [P, DV], f32)
    assert end[0] <= BIG + 40960
    rq_tok = at("rq_tok", [P, 2, TT, DK], f32, FREE)
    rk_tok = after("rk_tok", [P, 2, TT, DK], f32)
    st_in = after("st_in", [P, 2, DV], f32)
    st_out = after("st_out", [P, 2, DV], f32)
    assert end[0] <= V_TOK + TT * DV * 4
    gate = at("gate", [P, 2, TT, COLS], f32, FREE)
    gffn = after("gffn", [P, D_MODEL], f32)
    gffn_col = after("gffn_col", [P, KC], f32)
    md, x2, h2 = od, ro, od
    zero_rows = at("zero_rows", [P, D_MODEL], f32, FREE)
    logit = at("logit", [P, TT, NG + NE], f32, FREE + 9216)
    r4 = after("r4", [P, 10, TT, 4], f32)
    r1 = after("r1", [P, 12, TT, 1], f32)
    r16 = after("r16", [P, 4, TT, NE], f32)
    prod, wt, posm, wt_rest = (r16[:, i] for i in range(4))
    sel = after("sel", [P, TT, NE], bf16)[:, :, :]
    slot_rhs = after("slot_rhs", [P, TT, NE, SR], bf16)
    slot_tmp = after("slot_tmp", [P, 3, NE], f32)
    slot_w = after("slot_w", [P, NE], f32)
    g_idx = after("g_idx", [P, NE], u32)
    s_idx = after("s_idx", [P, NE], u32)
    g_cur, s_cur = after("g_cur", [P, 1], u32), after("s_cur", [P, 1], u32)
    w_cur = after("w_cur", [P, 1], f32)
    cmax = after("cmax", [P, 8], f32)
    npass = after("npass", [1, 1], i32)
    onehot = after("onehot", [P, 4, TT, P], bf16)
    assert end[0] <= FREE + 20480
    x_hi = at("x_hi", [P, KC, P], f32r, REGION)
    x_lo = after("x_lo", [P, KC, P], f32r)
    a_hi = after("a_hi", [P, FK, P], f32r)
    a_lo = after("a_lo", [P, FK, P], f32r)
    x_exp = after("x_exp", [P, D_MODEL], f32)
    silu = after("silu", [P, D_FF], f32)
    act_t = after("act_t", [P, D_FF], f32)
    y_exp = after("y_exp", [P, D_MODEL], f32)
    w_lo2 = after("w_lo2", [P, SPL, BLK], f32r)
    assert end[0] <= FREE + 9216
    w_hi2 = at("w_hi2", [P, SPL, BLK], f32r, BIG)

    ps = nc.alloc_psum_tensor("ps", [P, 8, COLS], f32)
    psf = ps[:, :, :].rearrange("p b c -> p (b c)")

    def scratch(name, rows, cols):
        return nc.dram_tensor(name, (rows, cols), f32, kind="Internal").ap()

    z = {"q": scratch("z_q", ROWS, D_MODEL), "rq": scratch("z_rq", ROWS, COLS), "rk": scratch("z_rk", ROWS, COLS),
         "rv": scratch("z_rv", ROWS, D_MODEL), "rg": scratch("z_rg", ROWS, D_MODEL),
         "gr": scratch("z_gr", ROWS, D_MODEL), "gd": scratch("z_gd", ROWS, D_MODEL),
         "k": o["k_new"], "v": o["v_new"]}
    h2_dram = scratch("h2_dram", ROWS, D_MODEL)
    y_dram = o["y"]

    def tiles(ap, c0, c1, t0=0, t1=TT):
        return ap[t0 * P:t1 * P, c0:c1].rearrange("(t p) c -> p t c", p=P)

    def sem(name):
        return nc.alloc_semaphore(name)

    raw_full = [sem(f"raw_full{s}") for s in range(RAW)]
    hi_ready, lo_ready, blocks_used = sem("hi_ready"), sem("lo_ready"), sem("blocks_used")
    gmix_in, gen_in, x_scaled = sem("gmix_in"), sem("gen_in"), sem("x_scaled")
    rot_in, ret_in, router_in = sem("rot_in"), sem("ret_in"), sem("router_in")
    x_in = [sem(f"x_in{t}") for t in range(TT)]
    x_padded, x_squared, ms_ready, rms_ready = sem("x_padded"), sem("x_squared"), sem("ms_ready"), sem("rms_ready")
    shi_ready, slo_ready = sem("shi_ready"), sem("slo_ready")
    act_step, dve_step, pool_step = sem("act_step"), sem("dve_step"), sem("pool_step")
    z_ready, z_evacuated, z_staged = sem("z_ready"), sem("z_evacuated"), sem("z_staged")
    stage_stored = [sem(f"stage_stored{i}") for i in range(3)]
    kq_in, lam_loaded = sem("kq_in"), sem("lam_loaded")
    v_in = [sem("v_in0"), sem("v_in1")]
    tr_ready, tr_evacuated = sem("tr_ready"), sem("tr_evacuated")
    lam_dots, lam_exps = sem("lam_dots"), sem("lam_exps")
    scores_ready, max_ready, exp_ready = sem("scores_ready"), sem("max_ready"), sem("exp_ready")
    mix_ready = sem("mix_ready")
    av_ready, o_squared, o_copied = sem("av_ready"), sem("o_squared"), sem("o_copied")
    ret_head_in = [sem("ret_head_in0"), sem("ret_head_in1")]
    rtr_ready, rtr_evacuated = sem("rtr_ready"), sem("rtr_evacuated")
    s_ready, s_decayed, kw_ready, qint_ready = sem("s_ready"), sem("s_decayed"), sem("kw_ready"), sem("qint_ready")
    ro_ready, ro_squared, ro_copied = sem("ro_ready"), sem("ro_squared"), sem("ro_copied")
    state_ready, state_evacuated, state_stored = sem("state_ready"), sem("state_evacuated"), sem("state_stored")
    src_ready, src_transposed = sem("src_ready"), sem("src_transposed")
    gate_in = [sem("gate_in0"), sem("gate_in1")]
    p_ready, p_evacuated = sem("p_ready"), sem("p_evacuated")
    h2_ready, wrs_ready, x2_squared = sem("h2_ready"), sem("wrs_ready"), sem("x2_squared")
    y_init, h2_stored, zero_ready = sem("y_init"), sem("h2_stored"), sem("zero_ready")
    logits_ready, route_act, route_dve = sem("logits_ready"), sem("route_act"), sem("route_dve")
    sel_ready, pos_ready, npass_ready = sem("sel_ready"), sem("pos_ready"), sem("npass_ready")
    onehot_ready, onehot_used, lists_ready = sem("onehot_ready"), sem("onehot_used"), sem("lists_ready")
    x_gathered, x_tr, xhi_ready, xlo_ready = sem("x_gathered"), sem("x_tr"), sem("xhi_ready"), sem("xlo_ready")
    silu_ready, act_ready = sem("silu_ready"), sem("act_ready")
    a_tr, ahi_ready, alo_ready = sem("a_tr"), sem("ahi_ready"), sem("alo_ready")
    y_evac, y_scattered, cur_ready = sem("y_evac"), sem("y_scattered"), sem("cur_ready")

    def chunk_block(n):
        c, half = divmod(n, BPC)
        if c < IN_CHUNKS:
            w, c0 = a["w_in"][0], SECTION[c][1]
        else:
            p, j = divmod(c - IN_CHUNKS, 2)
            w, c0 = a[("w_diff_o", "w_ret_o", "w_out")[p]][0], j * COLS
        return w[half * 512:(half + 1) * 512, c0:c0 + COLS].rearrange("(k p) c -> p k c", p=P)


    def raw_view(n, k):
        return raw[:, n % RAW, :].rearrange("p (k c) -> p k c", k=k)

    PASS0 = N0 - 2
    assert PASS0 % RAW == 0 and EB % RAW == 0 and RAW % SPL == 0 and PASS_BLOCKS % RAW == 0

    def number(j, i, q):
        return PASS0 + PASS_BLOCKS * j + EB * i + q

    def hi_of(q):
        return w_hi[:, q % SPL, :] if q % RAW < SPL or q < 0 else w_hi2[:, q % SPL, :]

    def lo_of(q):
        return w_lo[:, q % SPL, :] if q % RAW < SPL or q < 0 else w_lo2[:, q % SPL, :]

    def split_hi(act, j, i, q):
        n = number(j, i, q)
        act.wait_ge(raw_full[q % RAW], 16 * (PASS0 // RAW + NE * j + i + q // RAW + 1))
        if isinstance(n, int) and n < N0 + 4:
            if n >= SPL:
                act.wait_ge(blocks_used, min(n - SPL + 1, N0))
        else:
            act.wait_ge(blocks_used, n - 2 * SPL + 1)
        nc.scalar.copy(hi_of(q), raw[:, q % RAW, :]).then_inc(hi_ready, 1)

    def split_lo(dve, j, i, q):
        dve.wait_ge(hi_ready, number(j, i, q) + 1)
        nc.vector.tensor_tensor(lo_of(q), raw[:, q % RAW, :], hi_of(q).bitcast(f32),
                                ALU.subtract).then_inc(lo_ready, 1)

    def wait_product(eng, ready, chunks_before, c, t):
        if t < TT - 1:
            eng.wait_ge(ready, (TT - 1) * (c - chunks_before) + t + 1)
        else:
            eng.wait_ge(blocks_used, BPC * (c + 1))

    def product(out, s_h, s_l, w_h, w_l, first, last):
        nc.tensor.matmul(out, s_h, w_h, start=first, stop=False)
        nc.tensor.matmul(out, s_l, w_h, start=False, stop=False)
        return nc.tensor.matmul(out, s_h, w_l, start=False, stop=last)

    def mix_uses(g):
        return 2 if g % TT == PT else 1

    def head_transposed(h):
        return HEAD_USES * (h + 1) + sum(mix_uses(g) for g in range(TT * h - 1))

    def unit_transposed(g):
        heads = min((g + 1) // TT, H - 1) + 1
        return HEAD_USES * heads + sum(mix_uses(u) for u in range(g + 1))

    def unit_width(t):
        return (t + 1) * P if t < PT else PAST + SAMPLE

    def scores_view(g):
        t = g % TT
        if t < PT:
            return ps[:, 2 * (g % 2):2 * (g % 2) + 2, 0:unit_width(t)]
        return psf[:, 0:4 * COLS].rearrange("p (m c) -> p m c", m=2)[:, :, 0:unit_width(t)]

    block = nc.Block()
    block.__enter__()

    @block.sync
    def _(sp):
        sp.dma_start(x_tok[:, 0, :], a["x_prompt"][0, 0:P, :]).then_inc(x_in[0], 16)
        sp.dma_start(gmix[:, :], a["g_mix"][0].partition_broadcast(P)).then_inc(gmix_in, 16)
        sp.dma_start(gen[:, :], a["c_gen"]).then_inc(gen_in, 16)
        for t in range(1, PT):
            sp.dma_start(x_tok[:, t, :], a["x_prompt"][0, t * P:(t + 1) * P, :]).then_inc(x_in[t], 16)
        sp.dma_start(raw_view(0, 4), chunk_block(0)).then_inc(raw_full[0], 16)
        sp.dma_start(x_tok[0:SAMPLE, PT, :], a["x_sample"][0]).then_inc(x_in[PT], 16)
        for n in range(1, N0):
            if n >= RAW:
                sp.wait_ge(lo_ready, n - RAW + 1)
            sp.dma_start(raw_view(n, 4), chunk_block(n)).then_inc(raw_full[n % RAW], 16)

        def expert_loads(base, i, q, kind, part):
            n = base + q
            sp.wait_ge(lo_ready, n - RAW + 1)
            w = a[kind][0]
            if kind == "w_down":
                src = w[bass.ds(i, 1), part * 256:(part + 1) * 256, :].rearrange("e (k p) c -> p (e k) c", p=P)
                dst = raw[:, q % RAW, :].rearrange("p (k c) -> p k c", k=2)
            else:
                src = w[bass.ds(i, 1), part * 512:(part + 1) * 512, :].rearrange("e (k p) c -> p (e k) c", p=P)
                dst = raw[:, q % RAW, :].rearrange("p (k c) -> p k c", k=4)
            sp.dma_start(dst, src).then_inc(raw_full[q % RAW], 16)

        def expert_body(base, i, up_gate=True, down=True):
            if up_gate:
                for q, (kind, part) in enumerate((("w_up", 0), ("w_up", 1), ("w_gate", 0), ("w_gate", 1))):
                    expert_loads(base, i, q, kind, part)
            if down:
                for part in range(2):
                    expert_loads(base, i - 1, 4 + part, "w_down", part)

        def expert_pass(first):
            for q, (kind, part) in enumerate((("w_up", 0), ("w_up", 1), ("w_gate", 0), ("w_gate", 1))):
                expert_loads(first - 2, 0, 2 + q, kind, part)
            with sp.Fori(1, NE) as i:
                expert_body(first - 2 + EB * i, i)
            for part in range(2):
                expert_loads(first - 2 + EB * NE, NE - 1, part, "w_down", part)

        expert_pass(N0)
        sp.wait_ge(npass_ready, 1)
        passes = sp.value_load(npass[0:1, 0:1], min_val=1, max_val=TT)
        with sp.If(passes > 1):
            with sp.Fori(1, passes) as j:
                expert_pass(N0 + PASS_BLOCKS * j)

    def store_states(pool, h):
        pool.wait_ge(state_evacuated, 2 * (h + 1))
        pool.dma_start(o["s_prompt"][h], st_out[:, 0, :]).then_inc(state_stored, 16)
        pool.dma_start(o["s_sample"][h], st_out[:, 1, :]).then_inc(state_stored, 16)

    @block.gpsimd
    def _(pool):
        own = Steps(pool, pool_step)
        dma = pool.dma_start
        pool.wait_ge(x_in[PT], 16)
        dma(rot[:, :, :, :], a["c_rot"].rearrange("p (a t c) -> p a t c", a=4, t=TT)).then_inc(rot_in, 16)
        dma(gq[:, :], a["g_q"][0].partition_broadcast(P)).then_inc(rot_in, 16)
        dma(gk[:, :], a["g_k"][0].partition_broadcast(P)).then_inc(rot_in, 16)
        dma(gret[:, :], a["g_ret"][0].partition_broadcast(P)).then_inc(rot_in, 16)
        dma(gsub[:, :], a["g_sub"][0].partition_broadcast(P)).then_inc(rot_in, 16)
        dma(r_bias[:, 0:NG], a["b_group"][0].partition_broadcast(P)).then_inc(rot_in, 16)
        dma(r_bias[:, NG:NG + NE], a["b_expert"][0].partition_broadcast(P)).then_inc(rot_in, 16)

        def load_keys(h):
            lo, up = h * DV, (h + 1) * DV
            dma(k_tok[:, 0:PT, :], tiles(z["k"], lo, up, 0, PT)).then_inc(kq_in, 16)
            dma(k_tok[0:SAMPLE, PT, :], z["k"][PROMPT:REAL, lo:up]).then_inc(kq_in, 16)
            dma(kc_tok[:, :, :], a["cache_k"][0, 0, :, h, :].rearrange("(t p) c -> p t c", p=P)).then_inc(kq_in, 16)
            dma(q_tok[:, :, :], tiles(z["q"], lo, up)).then_inc(kq_in, 16)

        def load_values(h):
            lo, up = h * DV, (h + 1) * DV
            dma(v_tok[:, h % 2, 0:PT, :], tiles(z["v"], lo, up, 0, PT)).then_inc(v_in[h % 2], 16)
            dma(v_tok[0:SAMPLE, h % 2, PT, :], z["v"][PROMPT:REAL, lo:up]).then_inc(v_in[h % 2], 16)

        def load_cached_values(h):
            dma(vc_tok[:, h % 2, :, :], a["cache_v"][0, 0, :, h, :].rearrange("(t p) c -> p t c", p=P))\
                .then_inc(v_in[h % 2], 16)

        for c, (kind, _, c0) in enumerate(SECTION):
            if c in DVE_CHUNKS:
                pool.wait_ge(z_staged, DVE_CHUNKS.index(c) + 1)
            else:
                pool.wait_ge(z_evacuated, TT * (c + 1))
            if kind in "kv":
                dma(tiles(z[kind], c0, c0 + COLS, 0, PT), stage[:, c % 3, 0:PT, :]).then_inc(stage_stored[c % 3], 16)
                dma(z[kind][PROMPT:REAL, c0:c0 + COLS], stage[0:SAMPLE, c % 3, PT, :])\
                    .then_inc(stage_stored[c % 3], 16)
            else:
                dma(tiles(z[kind], c0, c0 + COLS), stage[:, c % 3, :, :]).then_inc(stage_stored[c % 3], 16)
            if c == DVE_CHUNKS[-1] + 1:
                for s in range(3):
                    pool.wait_ge(stage_stored[s], stored(5, s))
                load_keys(0)
                load_values(0)
                for n, name in enumerate(("lambda_q1", "lambda_k1", "lambda_q2", "lambda_k2")):
                    dma(lam_in[:, n, :], a[name][0].partition_broadcast(P)).then_inc(lam_loaded, 16)
                dma(hide[:, :], a["c_hide"]).then_inc(lam_loaded, 16)
        for s in range(3):
            pool.wait_ge(stage_stored[s], stored(IN_CHUNKS - 1, s))

        load_cached_values(0)
        for h in range(1, H):
            pool.wait_ge(tr_evacuated, head_transposed(h - 1))
            load_keys(h)
            if h >= 2:
                pool.wait_ge(av_ready, TT * (h - 1))
            load_values(h)
            load_cached_values(h)

        pool.wait_ge(tr_evacuated, head_transposed(H - 1))
        pool.wait_ge(av_ready, TT * (H - 1))
        c_ret = a["c_ret"]
        for h in range(H):
            if h == 1:
                pool.wait_ge(av_ready, UNITS)
            elif h >= 2:
                pool.wait_ge(state_evacuated, 2 * (h - 1))
            got = ret_head_in[h % 2]
            dma(rq_tok[:, h % 2, :, :], tiles(z["rq"], h * DK, (h + 1) * DK)).then_inc(got, 16)
            dma(rk_tok[:, h % 2, :, :], tiles(z["rk"], h * DK, (h + 1) * DK)).then_inc(got, 16)
            if h == 0:
                dma(decay[:, :, :], c_ret[:, 0:H * COLS].rearrange("p (h c) -> p h c", h=H)).then_inc(ret_in, 16)
                dma(inter[:, :, :], c_ret[:, H * COLS:H * COLS + H * P].rearrange("p (h c) -> p h c", h=H))\
                    .then_inc(ret_in, 16)
                dma(wk[:, :, :], c_ret[:, H * COLS + H * P:].rearrange("p (t h) -> p t h", h=H)).then_inc(ret_in, 16)
            dma(rv_tok[:, h % 2, :, :], tiles(z["rv"], h * DV, (h + 1) * DV)).then_inc(got, 16)
            dma(st_in[:, h % 2, :], a["state_ret"][0, 0, h]).then_inc(got, 16)
            if h >= 1:
                store_states(pool, h - 1)
        store_states(pool, H - 1)
        pool.wait_ge(state_stored, 32 * H)
        pool.wait_ge(ro_squared, UNITS)

        dma(gffn[:, :], a["g_ffn"][0].partition_broadcast(P)).then_inc(router_in, 16)
        for n, kind in enumerate(("rg", "rg", "gd", "gd", "gr", "gr", "x", "x")):
            if n == 2:
                dma(w_r[:, :, 0:NG], a["w_group"][0].rearrange("(k p) c -> p k c", p=P)).then_inc(router_in, 16)
                dma(gffn_col[:, :], a["g_ffn_col"]).then_inc(router_in, 16)
                dma(w_r[:, :, NG:NG + NE], a["w_expert"][0].rearrange("(k p) c -> p k c", p=P)).then_inc(router_in, 16)
            if n in (2, 3):
                pool.wait_ge(src_ready, 3 * TT)
            elif n >= 4:
                pool.wait_ge(p_evacuated, TT * (n - 3))
            c0, got = (n % 2) * COLS, gate_in[n % 2]
            if kind == "x":
                dma(gate[:, n % 2, 0:PT, :], tiles(a["x_prompt"][0], c0, c0 + COLS, 0, PT)).then_inc(got, 16)
                dma(gate[0:SAMPLE, n % 2, PT, :], a["x_sample"][0][:, c0:c0 + COLS]).then_inc(got, 16)
            else:
                dma(gate[:, n % 2, :, :], tiles(z[kind], c0, c0 + COLS)).then_inc(got, 16)

        pool.wait_ge(zero_ready, 1)
        dma(y_dram[SINK:SINK + P, :], zero_rows[:, :]).then_inc(y_init, 16)
        pool.wait_ge(p_evacuated, TT * OUT_CHUNKS)
        dma(tiles(y_dram, 0, D_MODEL), x2[:, :, :]).then_inc(y_init, 16)
        pool.wait_ge(y_init, 32)

        def pool_split(q):
            pool.wait_ge(hi_ready, PASS0 + q + 1)
            nc.gpsimd.tensor_tensor(lo_of(q), raw[:, q % RAW, :], hi_of(q).bitcast(f32), ALU.subtract)\
                .then_inc(lo_ready, 1)

        pool_split(2)
        pool.wait_ge(h2_ready, TT)
        dma(tiles(h2_dram, 0, D_MODEL), h2[:, :, :]).then_inc(h2_stored, 16)
        pool_split(3)
        pool_split(4)
        pool.wait_ge(h2_stored, 16)

        def gather(i, e):
            own(nc.gpsimd.tensor_copy(g_cur[:, :], g_idx[:, bass.ds(i, 1)]))
            pool.indirect_dma_start(out=x_exp[:, :], out_offset=None, in_=h2_dram,
                                    in_offset=bass.IndirectOffsetOnAxis(ap=g_cur[:, :], axis=0))\
                .then_inc(x_gathered, 16)

        def scatter(i, e):
            own(nc.gpsimd.tensor_copy(s_cur[:, :], s_idx[:, bass.ds(i, 1)]))
            nc.gpsimd.tensor_copy(w_cur[:, :], slot_w[:, bass.ds(i, 1)]).then_inc(cur_ready, 1)
            pool.wait_ge(y_evac, 2 * (e + 1))
            pool.indirect_dma_start(out=y_dram, out_offset=bass.IndirectOffsetOnAxis(ap=s_cur[:, :], axis=0),
                                    in_=y_exp[:, :], in_offset=None, compute_op=ALU.add).then_inc(y_scattered, 16)
            pool.wait_ge(y_scattered, 16 * (e + 1))

        def expert_pass(j):
            e0 = NE * j
            pool.wait_ge(lists_ready, 2 * j + 1)
            gather(0, e0)
            if j == 0:
                pool_split(5)
            pool.wait_ge(x_tr, 2 * (e0 + 1))
            gather(1, e0 + 1)
            pool.wait_ge(lists_ready, 2 * j + 2)
            for i in range(1, NE - 1):
                pool.wait_ge(x_tr, 2 * (e0 + i + 1))
                gather(i + 1, e0 + i + 1)
                if i >= 2:
                    scatter(i - 2, e0 + i - 2)
            scatter(NE - 3, e0 + NE - 3)
            scatter(NE - 2, e0 + NE - 2)
            scatter(NE - 1, e0 + NE - 1)

        expert_pass(0)
        pool.wait_ge(npass_ready, 1)
        passes = pool.value_load(npass[0:1, 0:1], min_val=1, max_val=TT)
        for j in range(1, TT):
            with pool.If(passes > j):
                expert_pass(j)

    @block.scalar
    def _(act):
        own = Steps(act, act_step)
        roots = [0]

        def root():
            roots[0] += 1
            act.wait_ge(ms_ready, roots[0])
            nc.scalar.activation(stat[:, 2, :, :], stat[:, 1, :, :], ACT.Sqrt).then_inc(rms_ready, 1)

        def source_hi(s, tiles_=range(TT)):
            for t in tiles_:
                for half in range(2):
                    u = 2 * TT * s + 2 * t + half
                    act.wait_ge(src_transposed, u + 1)
                    nc.scalar.copy(s_hi[:, 4 * half:4 * half + 4, t * P:(t + 1) * P],
                                   ps[:, 5 + u % 3, :].rearrange("p (k c) -> p k c", k=4)).then_inc(shi_ready, 1)

        source_hi(0, [0, 1, 2])
        split_hi(act, 0, 0, 0 - PASS0)
        source_hi(0, [3, 4])
        split_hi(act, 0, 0, 1 - PASS0)
        act.wait_ge(x_padded, 1)
        for t in range(TT):
            act.wait_ge(x_in[t], 16)
            if t:
                act.wait_ge(x_squared, t)
            nc.scalar.activation(stage[:, 0, 0:2, :].rearrange("p t c -> p (t c)"), x_tok[:, t, :], ACT.Square,
                                 accum_out=stat[:, 0, t, 0:1]).then_inc(x_squared, 1)
        root()
        split_hi(act, 0, 0, 2 - PASS0)
        act.wait_ge(x_squared, TT)
        act.wait_ge(x_scaled, 1)

        for c, (kind, _, _) in enumerate(SECTION):
            split_hi(act, 0, 0, 2 * c + 3 - PASS0)
            if c >= 3:
                act.wait_ge(stage_stored[c % 3], stored(c - 3, c % 3))
            func = {"rg": ACT.Silu, "gr": ACT.Sigmoid, "gd": ACT.Sigmoid}.get(kind, ACT.Copy)
            for t in range(TT):
                u = TT * c + t
                wait_product(act, z_ready, 0, c, t)
                nc.scalar.activation(stage[:, c % 3, t, :], ps[:, u % 8, :], func,
                                     scale=x_rstd[:, t:t + 1]).then_inc(z_evacuated, 1)
            if 2 * c + 4 < N0:
                split_hi(act, 0, 0, 2 * c + 4 - PASS0)
            if kind in ("k", "q"):
                root()

        uses = [0]

        def evacuate(pairs):
            act.wait_ge(tr_ready, uses[0] + 1)
            for n, (dst, src) in enumerate(pairs):
                ins = nc.scalar.copy(dst, src)
                if n == len(pairs) - 1:
                    ins.then_inc(tr_evacuated, 1)
                else:
                    ins.then_inc(act_step, 1)
                    own.n += 1
            uses[0] += 1

        for g in range(UNITS + 2):
            if g < UNITS and g % TT == 0:
                hb = (g // TT) % 2
                for m in range(2):
                    for dst in (kT[hb][:, m, 0:PROMPT], kT[hb][:, m, PROMPT:PROMPT + PAST], qT[hb][:, m, 0:PROMPT]):
                        evacuate([(dst, ps[:, 4 + uses[0] % 2, :])])
                bank = ps[:, 4 + uses[0] % 2, :]
                evacuate([(kT[hb][:, :, PROMPT + PAST:KEYS], bank[:, 0:2 * SAMPLE].rearrange("p (m c) -> p m c", m=2)),
                          (qT[hb][:, :, PROMPT:ROWS], bank[:, P:3 * P].rearrange("p (m c) -> p m c", m=2))])
            if g == 0:
                act.wait_ge(lam_dots, 1)
                nc.scalar.activation(lam[:, 2:4], lam[:, 0:2], ACT.Exp).then_inc(lam_exps, 1)
            if g < UNITS:
                act.wait_ge(max_ready, g + 1)
                width = unit_width(g % TT)
                for m in range(2):
                    nc.scalar.activation(prob[:, g % 2, m, 0:width], scores_view(g)[:, m, :], ACT.Exp,
                                         bias=neg_max[:, g, m:m + 1], scale=SC,
                                         accum_out=sums[:, g, m:m + 1]).then_inc(exp_ready, 1)
            if g == 1:
                for s in range(3):
                    act.wait_ge(stage_stored[s], stored(IN_CHUNKS - 1, s))
            if 1 <= g <= UNITS:
                u = g - 1
                n = min(u % TT + 1, PT)
                evacuate([(aT[:, u % 2, 0:n, :], ps[:, 4 + uses[0] % 2, 0:n * P].rearrange("p (k c) -> p k c", k=n))])
                if u % TT == PT:
                    evacuate([(aT[0:SAMPLE, u % 2, PT, :], ps[0:SAMPLE, 4 + uses[0] % 2, 0:P])])
            if g >= 2:
                u = g - 2
                act.wait_ge(o_copied, u + 1)
                if u:
                    act.wait_ge(o_squared, u)
                nc.scalar.activation(sq_att[:, :], od[:, u % TT, u // TT * DV:(u // TT + 1) * DV], ACT.Square,
                                     accum_out=stat[:, 0, u % TT, u // TT:u // TT + 1]).then_inc(o_squared, 1)
        root()

        for h in range(H):
            if h:
                act.wait_ge(qint_ready, h)
            for k, (dst, cols) in enumerate(((rqT[:, 0:PROMPT], PROMPT), (rkT[:, 0:PROMPT], PROMPT))):
                act.wait_ge(rtr_ready, 3 * h + k + 1)
                nc.scalar.copy(dst, ps[:, (3 * h + k) % 2, 0:cols]).then_inc(rtr_evacuated, 1)
            act.wait_ge(rtr_ready, 3 * h + 3)
            last = ps[:, (3 * h + 2) % 2, :]
            own.n += 1
            nc.scalar.copy(rqT[:, PROMPT:ROWS], last[:, 0:P]).then_inc(act_step, 1)
            nc.scalar.copy(rkT[:, PROMPT:ROWS], last[:, P:2 * P]).then_inc(rtr_evacuated, 1)
            for t in range(TT):
                u = TT * h + t
                act.wait_ge(ro_copied, u + 1)
                if u:
                    act.wait_ge(ro_squared, u)
                nc.scalar.activation(sq_ret[:, :], ro[:, t, h * DV:(h + 1) * DV], ACT.Square,
                                     accum_out=stat[:, 4, t, h:h + 1]).then_inc(ro_squared, 1)

        for p in range(3):
            source_hi(1 + p)
            if p == 0:
                root()
            first, last = 2 * (IN_CHUNKS + 2 * p) + (3 if p == 0 else 2), 2 * (IN_CHUNKS + 2 * p) + 5
            for n in range(first, min(last, N0 - 1) + 1):
                split_hi(act, 0, 0, n - PASS0)

        act.wait_ge(p_evacuated, TT * (OUT_CHUNKS - 1) + 3)
        for t in range(TT):
            source_hi(4, [t])
            for u in ([0], [1], [2, 3], [4], [])[t]:
                act.wait_ge(p_evacuated, TT * (OUT_CHUNKS - 1) + u + 1)
                if u:
                    act.wait_ge(x2_squared, u)
                nc.scalar.activation(psf[:, COLS:3 * COLS], x2[:, u, :], ACT.Square,
                                     accum_out=stat[:, 0, u, 0:1]).then_inc(x2_squared, 1)
            if t == 3:
                root()
        split_hi(act, 0, 0, 2)

        for k in range(2):
            act.wait_ge(route_dve, k + 1)
            nc.scalar.activation(r4[:, 2 * k + 1], r4[:, 2 * k], ACT.Exp).then_inc(route_act, 1)

        def x_parts(i, e):
            for half in range(2):
                act.wait_ge(x_tr, 2 * e + half + 1)
                nc.scalar.copy(x_hi[:, 4 * half:4 * half + 4, :],
                               ps[:, 5 + half, :].rearrange("p (k c) -> p k c", k=4)).then_inc(xhi_ready, 1)

        def gate_silu(j, i, e):
            act.wait_ge(blocks_used, number(j, i, 4 if not isinstance(i, int) or i > 0 else 6))
            nc.scalar.activation(silu[:, :], ps[:, 0, :], ACT.Silu).then_inc(silu_ready, 1)

        def act_hi(e):
            act.wait_ge(a_tr, e + 1)
            nc.scalar.copy(a_hi[:, :, :], ps[:, 4, :].rearrange("p (k c) -> p k c", k=FK)).then_inc(ahi_ready, 1)

        def weigh(j, step, q_end, e):
            act.wait_ge(blocks_used, number(j, step, q_end))
            act.wait_ge(cur_ready, e + 1)
            for c in range(2):
                nc.scalar.activation(y_exp[:, c * COLS:(c + 1) * COLS], ps[:, 2 + c, :], ACT.Copy,
                                     scale=w_cur[:, 0:1]).then_inc(y_evac, 1)

        def step(j, i, last=False):
            e = NE * j + i
            act_hi(e - 1)
            for q in (6, 7) if last else (6, 7, 8):
                split_hi(act, j, i, q)
            gate_silu(j, i, e)
            if not last:
                x_parts(i + 1, e + 1)
                for q in (9, 10, 11):
                    split_hi(act, j, i, q)
            weigh(j, i, 6, e - 1)

        def expert_pass(j):
            for q in range(3 if isinstance(j, int) else 2, 8):
                split_hi(act, j, 0, q)
            x_parts(0, NE * j)
            for q in (8, 9, 10):
                split_hi(act, j, 0, q)
            gate_silu(j, 0, NE * j)
            x_parts(1, NE * j + 1)
            split_hi(act, j, 0, 11)
            with act.Fori(1, NE - 1) as i:
                step(j, i)
            step(j, NE - 1, last=True)
            act_hi(NE * j + NE - 1)
            weigh(j, NE, 2, NE * j + NE - 1)

        act.wait_ge(logits_ready, TT)
        act.wait_ge(y_init, 32)
        expert_pass(0)
        act.wait_ge(npass_ready, 1)
        passes = act.value_load(npass[0:1, 0:1], min_val=1, max_val=TT)
        with act.If(passes > 1):
            with act.Fori(1, passes) as j:
                expert_pass(j)

    @block.vector
    def _(dve):
        own = Steps(dve, dve_step)
        v = nc.vector
        roots = [0]

        def ask_root(src, count):
            roots[0] += 1
            v.tensor_scalar(stat[:, 1, :, :], src, 1.0 / count, EPS, ALU.mult, ALU.add).then_inc(ms_ready, 1)

        def take_root():
            dve.wait_ge(rms_ready, roots[0])
            own(v.reciprocal(stat[:, 3, :, :], stat[:, 2, :, :]))

        def source_lo(s, t):
            for half in range(2):
                u = 2 * TT * s + 2 * t + half
                dve.wait_ge(shi_ready, u + 1)
                part = slice(4 * half, 4 * half + 4), slice(t * P, (t + 1) * P)
                v.tensor_tensor(s_lo[:, part[0], part[1]], ps[:, 5 + u % 3, :].rearrange("p (k c) -> p k c", k=4),
                                s_hi[:, part[0], part[1]].bitcast(f32), ALU.subtract).then_inc(slo_ready, 1)

        own(v.memset(stat[:, :, :, :], 1.0))
        v.memset(x_tok[SAMPLE:P, PT, :], 0.0).then_inc(x_padded, 1)

        def gained(t):
            dve.wait_ge(x_in[t], 16)
            if t == PT:
                dve.wait_ge(x_padded, 1)
            if t >= 2:
                dve.wait_ge(src_transposed, 2 * (t - 1))
            v.tensor_tensor(h_tok[:, t % 2, :], x_tok[:, t, :], gmix[:, :], ALU.mult).then_inc(src_ready, 1)

        dve.wait_ge(gmix_in, 16)
        gained(0)
        for t in range(1, TT):
            gained(t)
            source_lo(0, t - 1)
        split_lo(dve, 0, 0, 0 - PASS0)
        source_lo(0, TT - 1)
        split_lo(dve, 0, 0, 1 - PASS0)
        dve.wait_ge(x_squared, TT)
        ask_root(stat[:, 0, :, :], D_MODEL)
        dve.wait_ge(rms_ready, roots[0])
        v.reciprocal(x_rstd[:, :], stat[:, 2, :, 0]).then_inc(x_scaled, 1)
        dve.wait_ge(src_ready, TT)
        split_lo(dve, 0, 0, 2 - PASS0)
        dve.wait_ge(gen_in, 16)
        own(v.tensor_copy(tri16[:, :], tri))
        own(v.tensor_copy(ones16[:, :], ones))
        dve.wait_ge(rot_in, 16 * 7)

        for c, (kind, _, _) in enumerate(SECTION):
            split_lo(dve, 0, 0, 2 * c + 3 - PASS0)
            zc = stage[:, c % 3, :, :]
            heads = zc.rearrange("p t (h c) -> p (t h) c", h=4)
            if c in DVE_CHUNKS[1:]:
                dve.wait_ge(z_staged, DVE_CHUNKS.index(c))
            if kind in ("k", "q"):
                for t in range(TT):
                    dve.wait_ge(z_evacuated, TT * c + t + 1)
                    own(v.tensor_tensor(sq_tmp[:, :], zc[:, t, :], zc[:, t, :], ALU.mult))
                    own(v.tensor_reduce(stat[:, 0, t, :], sq_tmp[:, :].rearrange("p (h c) -> p h c", h=4),
                                        AX.X, ALU.add))
                ask_root(stat[:, 0, :, :], DK)
            if kind in ("rq", "rk"):
                tab = 0 if kind == "rq" else 2
                for t in range(TT):
                    dve.wait_ge(z_evacuated, TT * c + t + 1)
                    zt = zc[:, t, :].rearrange("p (h c) -> p h c", h=4)
                    x_a, x_b = zt[:, :, 0:DK // 2], zt[:, :, DK // 2:DK]
                    cos, sin = (rot[:, tab + k, t:t + 1, :].to_broadcast([P, H, DK // 2]) for k in range(2))
                    v.tensor_tensor(rot_tmp[:, 0], x_a, cos, ALU.mult).then_inc(dve_step, 1)
                    v.tensor_tensor(rot_tmp[:, 1], x_b, sin, ALU.mult).then_inc(dve_step, 1)
                    v.tensor_tensor(rot_tmp[:, 2], x_a, sin, ALU.mult).then_inc(dve_step, 1)
                    own.n += 3
                    own(v.tensor_tensor(rot_tmp[:, 3], x_b, cos, ALU.mult))
                    v.tensor_tensor(x_a, rot_tmp[:, 0], rot_tmp[:, 1], ALU.subtract).then_inc(dve_step, 1)
                    own.n += 1
                    last = v.tensor_tensor(x_b, rot_tmp[:, 2], rot_tmp[:, 3], ALU.add)
                    if t < TT - 1:
                        own(last)
                    else:
                        last.then_inc(z_staged, 1)
            if 2 * c + 4 < N0:
                split_lo(dve, 0, 0, 2 * c + 4 - PASS0)
            if kind in ("k", "q"):
                gain = gk if kind == "k" else gq
                take_root()
                rstd = stat[:, 3, :, :].rearrange("p t (h o) -> p (t h) o", o=1).to_broadcast([P, TT * H, DK])
                own(v.tensor_tensor(heads, heads, rstd, ALU.mult))
                v.tensor_tensor(heads, heads, gain[:, :].unsqueeze(1).to_broadcast([P, TT * H, DK]),
                                ALU.mult).then_inc(z_staged, 1)

        dve.wait_ge(lam_loaded, 80)
        own(v.tensor_tensor(lam_in[:, 0::2, :], lam_in[:, 0::2, :], lam_in[:, 1::2, :], ALU.mult))
        v.tensor_reduce(lam[:, 0:2], lam_in[:, 0::2, :], AX.X, ALU.add).then_inc(lam_dots, 1)
        dve.wait_ge(lam_exps, 1)
        own(v.tensor_tensor(lam[:, 0:1], lam[:, 2:3], lam[:, 3:4], ALU.subtract))
        own(v.tensor_scalar(lam[:, 1:2], lam[:, 0:1], LAM_INIT, None, ALU.add))

        for g in range(UNITS + 2):
            if 1 <= g <= UNITS:
                u = g - 1
                width = unit_width(u % TT)
                dve.wait_ge(exp_ready, 2 * (u + 1))
                p1, p2 = prob[:, u % 2, 0, 0:width], prob[:, u % 2, 1, 0:width]
                own(v.reciprocal(coef[:, u, :], sums[:, u, :]))
                own(v.tensor_tensor(coef[:, u, 1:2], coef[:, u, 1:2], lam[:, 1:2], ALU.mult))
                own(v.tensor_scalar(p2, p2, coef[:, u, 1:2], None, ALU.mult))
                v.scalar_tensor_tensor(p1, p1, coef[:, u, 0:1], p2, ALU.mult, ALU.subtract).then_inc(mix_ready, 1)
            if g < UNITS:
                dve.wait_ge(scores_ready, g + 1)
                own(v.tensor_reduce(neg_max[:, g, :], scores_view(g), AX.X, ALU.max))
                v.tensor_scalar(neg_max[:, g, :], neg_max[:, g, :], -SC, None, ALU.mult).then_inc(max_ready, 1)
            if g >= 2:
                u = g - 2
                h, t = divmod(u, TT)
                dve.wait_ge(av_ready, u + 1)
                if u == 0:
                    for s in range(3):
                        dve.wait_ge(stage_stored[s], stored(IN_CHUNKS - 1, s))
                v.tensor_copy(od[:, t, h * DV:(h + 1) * DV], ps[:, 6 + u % 2, 0:DV]).then_inc(o_copied, 1)
        dve.wait_ge(o_squared, UNITS)
        ask_root(stat[:, 0, :, :], DV)
        take_root()
        own(v.tensor_scalar(stat[:, 3, :, :], stat[:, 3, :, :], 1.0 - LAM_INIT, None, ALU.mult))

        def head_norm(dst, t, gain):
            for h in range(H):
                part = dst[:, t, h * DV:(h + 1) * DV]
                ins = v.scalar_tensor_tensor(part, part, stat[:, 3, t, h:h + 1], gain[:, :], ALU.mult, ALU.mult)
                yield ins

        def norm_attention(t):
            for h, ins in enumerate(head_norm(od, t, gsub)):
                if h < H - 1:
                    own.n += 1
                    ins.then_inc(dve_step, 1)
                else:
                    ins.then_inc(src_ready, 1)

        dve.wait_ge(o_copied, UNITS)
        norm_attention(PT)
        dve.wait_ge(ret_in, 48)
        for h in range(H):
            dve.wait_ge(ret_head_in[h % 2], 64 * (h // 2 + 1))
            v.tensor_tensor(kw[:, :, :], rk_tok[:, h % 2, :, :], wk[:, :, h:h + 1].to_broadcast([P, TT, DK]),
                            ALU.mult).then_inc(kw_ready, 1)
            norm_attention(h)
            dve.wait_ge(rtr_evacuated, 3 * (h + 1))
            v.tensor_tensor(q_int[:, :], rqT[:, PROMPT:ROWS], inter[:, h, :], ALU.mult).then_inc(qint_ready, 1)
            for m in range(TT):
                rows, width = (P, PROMPT - m * P) if m < PT else (SAMPLE, P)
                u = TT * h + m
                dve.wait_ge(s_ready, u + 1)
                v.tensor_tensor(sT[0:rows, ST_OFF[m]:ST_OFF[m] + width], ps[0:rows, 2 + u % 2, 0:width],
                                decay[0:rows, h, 0:width], ALU.mult).then_inc(s_decayed, 1)
            for t in range(TT):
                u = TT * h + t
                dve.wait_ge(ro_ready, u + 1)
                v.tensor_copy(ro[:, t, h * DV:(h + 1) * DV], ps[:, 4 + u % 2, 0:DV]).then_inc(ro_copied, 1)
            if h:
                dve.wait_ge(state_stored, 32 * h)
            dve.wait_ge(state_ready, 2 * h + 1)
            v.tensor_copy(st_out[:, 0, :], ps[:, 6, 0:DV]).then_inc(state_evacuated, 1)
            dve.wait_ge(state_ready, 2 * h + 2)
            v.scalar_tensor_tensor(st_out[:, 1, :], st_in[:, h % 2, :], GAMMA[h] ** SAMPLE, ps[:, 7, 0:DV],
                                   ALU.mult, ALU.add).then_inc(state_evacuated, 1)

        for t in range(TT):
            source_lo(1, t)
        dve.wait_ge(ro_squared, UNITS)
        dve.wait_ge(ro_copied, UNITS)
        ask_root(stat[:, 4, :, :], DV)
        take_root()
        for t in range(TT):
            for ins in head_norm(ro, t, gret):
                own(ins)
            for c in range(2):
                dve.wait_ge(gate_in[c], 16)
                part = ro[:, t, c * COLS:(c + 1) * COLS]
                ins = v.tensor_tensor(part, part, gate[:, c, t, :], ALU.mult)
                ins.then_inc(*((dve_step, 1) if c == 0 else (src_ready, 1)))
            own.n += 1

        def gate_value(n):
            return 16 * (n // 2 + 1) if n < 6 else 80

        for p in range(3):
            if p == 1:
                dve.wait_ge(router_in, 64)
                dve.wait_ge(src_ready, 2 * TT)
                own(v.tensor_tensor(w_r[:, :, :], w_r[:, :, :], gffn_col[:, :].unsqueeze(2).to_broadcast([P, KC, NR]),
                                    ALU.mult))
                own(v.tensor_copy(w_rs[:, :, 0:NR], w_r[:, :, :]))
                v.tensor_tensor(w_rs[:, :, NR:2 * NR], w_r[:, :, :], w_rs[:, :, 0:NR].bitcast(f32), ALU.subtract)\
                    .then_inc(wrs_ready, 1)
            if p:
                for t in range(TT):
                    source_lo(1 + p, t)
                split_lo(dve, 0, 0, 2 * (IN_CHUNKS + 2 * p) + 2 - PASS0)
            for j in range(2):
                c = IN_CHUNKS + 2 * p + j
                if 2 * c + 3 < N0:
                    split_lo(dve, 0, 0, 2 * c + 3 - PASS0)
                dve.wait_ge(gate_in[j], gate_value(2 + 2 * p + j))
                for t in range(TT):
                    wait_product(dve, p_ready, IN_CHUNKS, c, t)
                    g_t, cols = gate[:, j, t, :], slice(j * COLS, (j + 1) * COLS)
                    if p == 0:
                        v.tensor_tensor(md[:, t, cols], ps[:, t, :], g_t, ALU.mult).then_inc(p_evacuated, 1)
                    elif p == 1:
                        own(v.tensor_tensor(g_t, ps[:, t, :], g_t, ALU.mult))
                        v.tensor_tensor(md[:, t, cols], md[:, t, cols], g_t, ALU.add).then_inc(p_evacuated, 1)
                    else:
                        v.tensor_tensor(x2[:, t, cols], ps[:, t, :], g_t, ALU.add).then_inc(p_evacuated, 1)
                if j == 0 and 2 * c + 4 < N0:
                    split_lo(dve, 0, 0, 2 * c + 4 - PASS0)
                if p == 2 and j == 0:
                    dve.wait_ge(p_evacuated, TT * (OUT_CHUNKS - 1))
                    v.memset(zero_rows[:, :], 0.0).then_inc(zero_ready, 1)

        def h2_tile(t):
            v.scalar_tensor_tensor(h2[:, t, :], x2[:, t, :], stat[:, 3, t, 0:1], gffn[:, :],
                                   ALU.mult, ALU.mult).then_inc(h2_ready, 1)

        for t in range(3):
            source_lo(4, t)
        dve.wait_ge(x2_squared, TT)
        ask_root(stat[:, 0, :, :], D_MODEL)
        source_lo(4, 3)
        take_root()
        h2_tile(0)
        h2_tile(1)
        source_lo(4, 4)
        for t in range(2, TT):
            h2_tile(t)
        own(v.tensor_copy(slot_rhs[:, :, :, 0], tile_row.unsqueeze(2).to_broadcast([P, TT, NE])))
        own(v.tensor_copy(slot_rhs[:, :, :, 1], tok_plus1[:, 0:1].unsqueeze(2).to_broadcast([P, TT, NE])))

        dve.wait_ge(logits_ready, TT)
        raw_l = ps[:, 0, 0:TT * 2 * NR].rearrange("p (t c) -> p t c", t=TT)
        own(v.tensor_copy(logit[:, :, :], raw_l[:, :, NR:2 * NR]))
        own(v.tensor_tensor(logit[:, :, :], logit[:, :, :], raw_l[:, :, 0:NR], ALU.add))
        own(v.tensor_tensor(logit[:, :, :], logit[:, :, :], stat[:, 3, :, 0:1].to_broadcast([P, TT, NR]), ALU.mult))
        own(v.tensor_tensor(logit[:, :, :], logit[:, :, :], r_bias[:, :].unsqueeze(1).to_broadcast([P, TT, NR]),
                            ALU.add))
        g_log = logit[:, :, 0:NG]
        e_log = logit[:, :, NG:NR].rearrange("p t (g e) -> p t g e", g=NG)

        def wide(ap):
            return ap.to_broadcast([P, TT, 4])

        def first_of(mask, values, top, rank):
            own(v.tensor_tensor(mask, values, wide(top), ALU.is_equal))
            own(v.tensor_tensor(mask, mask, earlier.unsqueeze(1).to_broadcast([P, TT, 4]), ALU.mult))
            own(v.tensor_reduce(rank, mask, AX.X, ALU.max))
            own(v.tensor_tensor(mask, mask, wide(rank), ALU.is_equal))

        own(v.tensor_reduce(r1[:, 0], g_log, AX.X, ALU.max))
        v.tensor_tensor(r4[:, 0], g_log, wide(r1[:, 0]), ALU.subtract).then_inc(route_dve, 1)
        g_mask = r4[:, 4]
        first_of(g_mask, g_log, r1[:, 0], r1[:, 1])
        prod4 = prod.rearrange("p t (g e) -> p t g e", g=NG)
        groups = g_mask.unsqueeze(3).to_broadcast([P, TT, NG, EPG])
        own(v.tensor_tensor(prod4, e_log, groups, ALU.mult))
        own(v.tensor_reduce(r4[:, 5], prod.rearrange("p t (g e) -> p t e g", g=NG), AX.X, ALU.add))
        own(v.tensor_reduce(r1[:, 2], r4[:, 5], AX.X, ALU.max))
        v.tensor_tensor(r4[:, 2], r4[:, 5], wide(r1[:, 2]), ALU.subtract).then_inc(route_dve, 1)
        dve.wait_ge(route_act, 1)
        own(v.tensor_reduce(r1[:, 3], r4[:, 1], AX.X, ALU.add))
        own(v.reciprocal(r1[:, 4], r1[:, 3]))
        dve.wait_ge(route_act, 2)
        e_p, first, second = r4[:, 3], r4[:, 6], r4[:, 7]
        own(v.tensor_reduce(r1[:, 5], e_p, AX.X, ALU.max))
        first_of(first, e_p, r1[:, 5], r1[:, 6])
        own(v.scalar_tensor_tensor(r4[:, 8], first, -2.0, e_p, ALU.mult, ALU.add))
        own(v.tensor_reduce(r1[:, 7], r4[:, 8], AX.X, ALU.max))
        first_of(second, r4[:, 8], r1[:, 7], r1[:, 8])
        own(v.tensor_tensor(r1[:, 9], r1[:, 5], r1[:, 7], ALU.add))
        own(v.reciprocal(r1[:, 10], r1[:, 9]))
        own(v.tensor_tensor(r1[:, 10], r1[:, 10], r1[:, 4], ALU.mult))
        own(v.tensor_tensor(r4[:, 9], first, second, ALU.add))
        own(v.tensor_tensor(r4[:, 8], e_p, r4[:, 9], ALU.mult))
        own(v.tensor_tensor(r4[:, 8], r4[:, 8], wide(r1[:, 10]), ALU.mult))
        own(v.tensor_tensor(r4[:, 9], r4[:, 9], wide(tok_valid.unsqueeze(2)), ALU.mult))
        sel4, wt4 = (x.rearrange("p t (g e) -> p t g e", g=NG) for x in (sel, wt))
        v.tensor_tensor(sel4, groups, r4[:, 9].unsqueeze(2).to_broadcast([P, TT, NG, EPG]), ALU.mult)\
            .then_inc(sel_ready, 1)
        own(v.tensor_tensor(wt4, groups, r4[:, 8].unsqueeze(2).to_broadcast([P, TT, NG, EPG]), ALU.mult))
        own(v.tensor_copy(slot_rhs[:, :, :, 2], wt))
        own(v.tensor_tensor(wt_rest, wt, slot_rhs[:, :, :, 2], ALU.subtract))
        own(v.tensor_copy(slot_rhs[:, :, :, 3], wt_rest))
        own(v.tensor_tensor(slot_rhs[:, :, :, 4], wt_rest, slot_rhs[:, :, :, 3], ALU.subtract))
        dve.wait_ge(sel_ready, 1)
        own(v.tensor_scalar(prod, sel, -1e6, 1e6, ALU.mult, ALU.add))
        dve.wait_ge(pos_ready, 1)
        own(v.tensor_tensor(posm, prod, ps[:, 6, 0:TT * NE].rearrange("p (t e) -> p t e", t=TT), ALU.add))

        own(v.tensor_reduce(cmax[:, 0:1], ps[:, 6, TT * NE:(TT + 1) * NE], AX.X, ALU.max))

        def count_passes():
            for k in range(1, TT):
                own(v.tensor_scalar(cmax[:, k:k + 1], cmax[:, 0:1], float(P * k), None, ALU.is_gt))
            own(v.tensor_reduce(cmax[:, 5:6], cmax[:, 1:TT], AX.X, ALU.add))
            v.tensor_scalar(npass[0:1, 0:1], cmax[0:1, 5:6], 1.0, None, ALU.add).then_inc(npass_ready, 1)

        LIST_STEPS = 10

        def finish_lists(j, e0, e1):
            dve.wait_ge(onehot_used, NE * j + e1)
            got = ps[:, 4 if e0 == 0 else 7, SR * e0:SR * e1].rearrange("p (e k) -> p e k", k=SR)
            row, empty, target = (slot_tmp[:, k, e0:e1] for k in range(3))
            own(v.tensor_reduce(row, got[:, :, 0:2], AX.X, ALU.add))
            own(v.tensor_scalar(g_idx[:, e0:e1], row, -1.0, 0.0, ALU.add, ALU.max))
            own(v.tensor_scalar(empty, row, 0.0, None, ALU.is_equal))
            own(v.scalar_tensor_tensor(target, empty, sink_plus1, row, ALU.mult, ALU.add))
            own(v.tensor_reduce(slot_w[:, e0:e1], got[:, :, 2:SR], AX.X, ALU.add))
            v.tensor_scalar(s_idx[:, e0:e1], target, -1.0, None, ALU.add).then_inc(lists_ready, 1)

        def lists(j):
            if not isinstance(j, int):
                dve.wait_ge(y_scattered, 16 * NE * j)
                own(v.tensor_scalar(posm, posm, -float(P), None, ALU.add))
            for e in range(NE):
                if e >= 4:
                    dve.wait_ge(onehot_used, NE * j + e - 3)
                v.tensor_tensor(onehot[:, e % 4, :, :], iota.unsqueeze(1).to_broadcast([P, TT, P]),
                                posm[:, :, e:e + 1].to_broadcast([P, TT, P]), ALU.is_equal).then_inc(onehot_ready, 1)
                if e in (1, NE - 1):
                    finish_lists(j, 0 if e == 1 else 2, e + 1)

        def x_parts(e):
            for half in range(2):
                dve.wait_ge(xhi_ready, 2 * e + half + 1)
                part = slice(4 * half, 4 * half + 4)
                v.tensor_tensor(x_lo[:, part, :], ps[:, 5 + half, :].rearrange("p (k c) -> p k c", k=4),
                                x_hi[:, part, :].bitcast(f32), ALU.subtract).then_inc(xlo_ready, 1)

        def gated(e):
            dve.wait_ge(silu_ready, e + 1)
            v.tensor_tensor(act_t[:, :], ps[:, 1, :], silu[:, :], ALU.mult).then_inc(act_ready, 1)

        def act_lo(e):
            dve.wait_ge(ahi_ready, e + 1)
            v.tensor_tensor(a_lo[:, :, :], ps[:, 4, :].rearrange("p (k c) -> p k c", k=FK),
                            a_hi[:, :, :].bitcast(f32), ALU.subtract).then_inc(alo_ready, 1)

        def step(j, i, last=False):
            e = NE * j + i
            act_lo(e - 1)
            for q in (6, 7) if last else (6, 7, 8):
                split_lo(dve, j, i, q)
            gated(e)
            if not last:
                x_parts(e + 1)
                for q in (9, 10, 11):
                    split_lo(dve, j, i, q)

        COUNT_STEPS = TT
        before = own.n

        def expert_pass(j):
            if not isinstance(j, int):
                own.base, own.n = (LIST_STEPS + 1) * (j - 1), before + LIST_STEPS + COUNT_STEPS
            lists(j)
            if isinstance(j, int):
                count_passes()
                dve.wait_ge(y_init, 32)
                dve.wait_ge(h2_stored, 16)
            x_parts(NE * j)
            if isinstance(j, int):
                dve.wait_ge(lo_ready, PASS0 + 2 + POOL_SPLITS)
            for q in range(2 + POOL_SPLITS if isinstance(j, int) else 2, 11):
                split_lo(dve, j, 0, q)
            gated(NE * j)
            x_parts(NE * j + 1)
            split_lo(dve, j, 0, 11)
            with dve.Fori(1, NE - 1) as i:
                step(j, i)
            step(j, NE - 1, last=True)
            act_lo(NE * j + NE - 1)

        expert_pass(0)
        assert own.n == before + LIST_STEPS + COUNT_STEPS
        passes = dve.value_load(npass[0:1, 0:1], min_val=1, max_val=TT)
        with dve.If(passes > 1):
            with dve.Fori(1, passes) as j:
                expert_pass(j)

    @block.tensor
    def _(pe):
        mm, transpose = nc.tensor.matmul, nc.tensor.transpose

        def source(s, src, ready, tiles_=range(TT)):
            for t in tiles_:
                ready(t)
                for half in range(2):
                    u = 2 * TT * s + 2 * t + half
                    if u >= 3:
                        pe.wait_ge(slo_ready, u - 2)
                    for k in range(4):
                        col = (4 * half + k) * P
                        last = transpose(ps[:, 5 + u % 3, k * P:(k + 1) * P], src(t)[:, col:col + P], ident)
                    last.then_inc(src_transposed, 1)

        def chunk(c, banks, free, ready):
            for half in range(BPC):
                n = 2 * c + half
                q = n - PASS0
                pe.wait_ge(lo_ready, n + 1)
                for kk in range(4):
                    k = 4 * half + kk
                    cols = slice(kk * COLS, (kk + 1) * COLS)
                    for t in range(TT):
                        if k == 0:
                            free(t)
                        rows = slice(t * P, (t + 1) * P)
                        last = product(banks(t), s_hi[:, k, rows], s_lo[:, k, rows], w_hi[:, q % SPL, cols],
                                       w_lo[:, q % SPL, cols], k == 0, k == KC - 1)
                        if k == KC - 1 and t < TT - 1:
                            last.then_inc(ready, 1)
                last.then_inc(blocks_used, 1)

        pe.wait_ge(gen_in, 16)
        source(0, lambda t: h_tok[:, t % 2, :], lambda t: pe.wait_ge(src_ready, t + 1))
        pe.wait_ge(slo_ready, 2 * TT)

        def in_free(c, t):
            if TT * c + t >= 8:
                pe.wait_ge(z_evacuated, TT * c + t - 7)

        for c in range(IN_CHUNKS):
            chunk(c, lambda t: ps[:, (TT * c + t) % 8, :], lambda t: in_free(c, t), z_ready)

        pe.wait_ge(z_evacuated, TT * IN_CHUNKS)
        pe.wait_ge(lam_loaded, 80)
        uses = [0]

        def transposes(parts):
            if uses[0] >= 2:
                pe.wait_ge(tr_evacuated, uses[0] - 1)
            bank = ps[:, 4 + uses[0] % 2, :]
            for out, src in parts:
                rows = src.shape[0]
                last = transpose(out(bank), src, ident[0:rows, 0:rows])
            last.then_inc(tr_ready, 1)
            uses[0] += 1

        def four(tile_of):
            return [(lambda bank, t=t: bank[:, t * P:(t + 1) * P], tile_of(t)) for t in range(PT)]

        def scores(g):
            h, t = divmod(g, TT)
            if t == PT or (t == 0 and g):
                pe.wait_ge(exp_ready, 2 * g)
            elif g >= 2:
                pe.wait_ge(exp_ready, 2 * (g - 1))
            hb, width = h % 2, unit_width(t)
            for m in range(2):
                q = qT[hb][:, m, t * P:(t + 1) * P]
                if t < PT:
                    out = ps[:, 2 * (g % 2) + m, 0:width]
                    mm(out, q, kT[hb][:, m, 0:width], start=True, stop=False)
                    last = mm(out[:, width - P:width], hide[0:1, 0:P], hide[0:1, P:2 * P],
                              start=False, stop=True)
                else:
                    mm(psf[:, 2 * m * COLS:2 * m * COLS + PAST], q, kT[hb][:, m, PROMPT:PROMPT + PAST],
                       start=True, stop=True)
                    last = mm(psf[:, 2 * m * COLS + PAST:2 * m * COLS + PAST + SAMPLE], q,
                              kT[hb][:, m, PROMPT + PAST:KEYS], start=True, stop=True)
            last.then_inc(scores_ready, 1)

        def transposed_mix(u):
            mixed = prob[:, u % 2, 0, :]
            pe.wait_ge(mix_ready, u + 1)
            n = min(u % TT + 1, PT)
            transposes(four(lambda k: mixed[:, k * P:(k + 1) * P])[0:n])
            if u % TT == PT:
                transposes([(lambda b: b[0:SAMPLE, 0:P], mixed[:, PAST:PAST + SAMPLE])])
            assert uses[0] == unit_transposed(u)

        def weighted_values(u):
            uh, ut = divmod(u, TT)
            if ut == 0:
                pe.wait_ge(v_in[uh % 2], 48 * (uh // 2 + 1))
            if u >= 2:
                pe.wait_ge(o_copied, u - 1)
            pe.wait_ge(tr_evacuated, unit_transposed(u))
            out = ps[:, 6 + u % 2, 0:DV]
            if ut < PT:
                for k in range(ut + 1):
                    last = mm(out, aT[:, u % 2, k, :], v_tok[:, uh % 2, k, :], start=k == 0, stop=k == ut)
            else:
                for k in range(PT):
                    mm(out, aT[:, u % 2, k, :], vc_tok[:, uh % 2, k, :], start=k == 0, stop=False)
                last = mm(out, aT[0:SAMPLE, u % 2, PT, :], v_tok[0:SAMPLE, uh % 2, PT, :],
                          start=False, stop=True)
            last.then_inc(av_ready, 1)

        for g in range(UNITS + 2):
            h, t = divmod(g, TT)
            if g < UNITS and t == 0:
                pe.wait_ge(kq_in, 64 * (h + 1))
                for m in range(2):
                    cols = slice(m * DK, (m + 1) * DK)
                    transposes(four(lambda t: k_tok[:, t, cols]))
                    transposes(four(lambda t: kc_tok[:, t, cols]))
                    transposes(four(lambda t: q_tok[:, t, cols]))
                transposes([(lambda b, m=m: b[:, m * SAMPLE:(m + 1) * SAMPLE],
                             k_tok[0:SAMPLE, PT, m * DK:(m + 1) * DK]) for m in range(2)] +
                           [(lambda b, m=m: b[:, (m + 1) * P:(m + 2) * P],
                             q_tok[:, PT, m * DK:(m + 1) * DK]) for m in range(2)])
                assert uses[0] == head_transposed(h)
                pe.wait_ge(tr_evacuated, head_transposed(h))
            if g < UNITS:
                scores(g)
            if 1 <= g <= UNITS:
                transposed_mix(g - 1)
            if g >= 2:
                weighted_values(g - 2)

        for h in range(H):
            hb = h % 2
            pe.wait_ge(ret_head_in[hb], 64 * (h // 2 + 1))
            if h == 0:
                pe.wait_ge(exp_ready, 2 * UNITS)
            for k, parts in enumerate(([(rq_tok, t) for t in range(PT)], [(rk_tok, t) for t in range(PT)],
                                       [(rq_tok, PT), (rk_tok, PT)])):
                u = 3 * h + k
                if u >= 2:
                    pe.wait_ge(rtr_evacuated, u - 1)
                for n, (src, t) in enumerate(parts):
                    last = transpose(ps[:, u % 2, n * P:(n + 1) * P], src[:, hb, t, :], ident)
                last.then_inc(rtr_ready, 1)
            pe.wait_ge(rtr_evacuated, 3 * (h + 1))
            for m in range(TT):
                u = TT * h + m
                if u >= 2:
                    pe.wait_ge(s_decayed, u - 1)
                rows, width = (P, PROMPT - m * P) if m < PT else (SAMPLE, P)
                mm(ps[0:rows, 2 + u % 2, 0:width], rkT[:, m * P:m * P + rows], rqT[:, m * P:m * P + width],
                   start=True, stop=True).then_inc(s_ready, 1)
            for t in range(TT):
                u = TT * h + t
                if h == 0 and t == 0:
                    pe.wait_ge(tr_evacuated, unit_transposed(UNITS - 1))
                if u >= 2:
                    pe.wait_ge(ro_copied, u - 1)
                out = ps[:, 4 + u % 2, 0:DV]
                if t < PT:
                    pe.wait_ge(s_decayed, TT * h + t + 1)
                    for m in range(t + 1):
                        at_ = ST_OFF[m] + (t - m) * P
                        last = mm(out, sT[:, at_:at_ + P], rv_tok[:, hb, m, :], start=m == 0, stop=m == t)
                else:
                    pe.wait_ge(s_decayed, TT * (h + 1))
                    pe.wait_ge(qint_ready, h + 1)
                    mm(out, sT[0:SAMPLE, ST_OFF[PT]:ST_OFF[PT] + P], rv_tok[0:SAMPLE, hb, PT, :],
                       start=True, stop=False)
                    last = mm(out, q_int[:, :], st_in[:, hb, :], start=False, stop=True)
                last.then_inc(ro_ready, 1)
            pe.wait_ge(kw_ready, h + 1)
            if h == 0:
                pe.wait_ge(o_copied, UNITS)
            else:
                pe.wait_ge(state_evacuated, 2 * h)
            for t in range(PT):
                last = mm(ps[:, 6, 0:DV], kw[:, t, :], rv_tok[:, hb, t, :], start=t == 0, stop=t == PT - 1)
            last.then_inc(state_ready, 1)
            mm(ps[:, 7, 0:DV], kw[0:SAMPLE, PT, :], rv_tok[0:SAMPLE, hb, PT, :], start=True, stop=True)\
                .then_inc(state_ready, 1)

        pe.wait_ge(state_evacuated, 2 * H)
        pe.wait_ge(ro_copied, UNITS)

        def out_free(x, t):
            if x:
                pe.wait_ge(p_evacuated, TT * (x - 1) + t + 1)

        for p, src in enumerate((od, ro, md)):
            if p < 2:
                source(1 + p, lambda t: src[:, t, :],
                       lambda t: pe.wait_ge(src_ready, TT * (1 + p) + (t + 1 if p else TT)))
            else:
                source(1 + p, lambda t: src[:, t, :], lambda t: pe.wait_ge(p_evacuated, TT * 3 + t + 1))
            pe.wait_ge(slo_ready, 2 * TT * (2 + p))
            for x in (2 * p, 2 * p + 1):
                chunk(IN_CHUNKS + x, lambda t: ps[:, t, :], lambda t: out_free(x, t), p_ready)

        pe.wait_ge(wrs_ready, 1)
        for t in range(TT + 1):
            if t < TT:
                source(4, lambda t: x2[:, t, :], lambda t: pe.wait_ge(p_evacuated, TT * (OUT_CHUNKS - 1) + t + 1), [t])
            if t >= 1:
                rows, out = slice((t - 1) * P, t * P), ps[:, 0, (t - 1) * 2 * NR:t * 2 * NR]
                pe.wait_ge(slo_ready, 2 * TT * 4 + 2 * t)
                for k in range(KC):
                    mm(out, s_hi[:, k, rows], w_rs[:, k, :], start=k == 0, stop=False)
                    last = mm(out, s_lo[:, k, rows], w_rs[:, k, :], start=False, stop=k == KC - 1)
                last.then_inc(logits_ready, 1)
        pe.wait_ge(sel_ready, 1)
        for t in range(TT):
            for s in range(t + 1):
                mm(ps[:, 6, t * NE:(t + 1) * NE], tri16[:, :] if s == t else ones16[:, :], sel[:, s, :],
                   start=s == 0, stop=s == t)
        for s in range(TT):
            last = mm(ps[:, 6, TT * NE:(TT + 1) * NE], ones16[:, :], sel[:, s, :], start=s == 0, stop=s == TT - 1)
        last.then_inc(pos_ready, 1)

        def lists(j):
            for e in range(NE):
                pe.wait_ge(onehot_ready, NE * j + e + 1)
                for t in range(TT):
                    last = mm(ps[:, 4 if e < 2 else 7, SR * e:SR * (e + 1)], onehot[:, e % 4, t, :],
                              slot_rhs[:, t, e, :], start=t == 0, stop=t == TT - 1)
                last.then_inc(onehot_used, 1)

        def rows_in(e, first=False):
            pe.wait_ge(x_gathered, 16 * (e + 1))
            if not first:
                pe.wait_ge(xlo_ready, 2 * e)
            for half in range(2):
                for k in range(4):
                    col = (4 * half + k) * P
                    last = transpose(ps[:, 5 + half, k * P:(k + 1) * P], x_exp[:, col:col + P], ident)
                last.then_inc(x_tr, 1)

        def up_gate(j, i, e, q0, first=False):
            pe.wait_ge(xlo_ready, 2 * (e + 1))
            if not first:
                pe.wait_ge(act_ready, e)
            for b in range(4):
                q = q0 + b
                pe.wait_ge(lo_ready, number(j, i, q) + 1)
                for kk in range(4):
                    k, cols = 4 * (b % 2) + kk, slice(kk * COLS, (kk + 1) * COLS)
                    last = product(ps[:, 1 - b // 2, :], x_hi[:, k, :], x_lo[:, k, :], hi_of(q)[:, cols],
                                   lo_of(q)[:, cols], k == 0, k == KC - 1)
                last.then_inc(blocks_used, 1)

        def acts_in(e):
            pe.wait_ge(act_ready, e + 1)
            for k in range(FK):
                last = transpose(ps[:, 4, k * P:(k + 1) * P], act_t[:, k * P:(k + 1) * P], ident)
            last.then_inc(a_tr, 1)

        def down(j, i, e, q0, first=False):
            pe.wait_ge(alo_ready, e + 1)
            if not first:
                pe.wait_ge(y_evac, 2 * e)
            for b in range(2):
                q = q0 + b
                pe.wait_ge(lo_ready, number(j, i, q) + 1)
                for kk in range(2):
                    for c in range(2):
                        k, cols = 2 * b + kk, slice((2 * kk + c) * COLS, (2 * kk + c + 1) * COLS)
                        last = product(ps[:, 2 + c, :], a_hi[:, k, :], a_lo[:, k, :], hi_of(q)[:, cols],
                                       lo_of(q)[:, cols], k == 0, k == FK - 1)
                last.then_inc(blocks_used, 1)

        def expert_pass(j):
            e0 = NE * j
            first = isinstance(j, int)
            lists(j)
            rows_in(e0, first)
            up_gate(j, 0, e0, 2, first)
            rows_in(e0 + 1)
            acts_in(e0)
            up_gate(j, 1, e0 + 1, 0)
            rows_in(e0 + 2)
            down(j, 1, e0, 4, first)
            with pe.Fori(2, NE - 1) as i:
                acts_in(e0 + i - 1)
                up_gate(j, i, e0 + i, 0)
                rows_in(e0 + i + 1)
                down(j, i, e0 + i - 1, 4)
            acts_in(e0 + NE - 2)
            up_gate(j, NE - 1, e0 + NE - 1, 0)
            down(j, NE - 1, e0 + NE - 2, 4)
            acts_in(e0 + NE - 1)
            down(j, NE, e0 + NE - 1, 0)

        expert_pass(0)
        pe.wait_ge(npass_ready, 1)
        passes = pe.value_load(npass[0:1, 0:1], min_val=1, max_val=TT)
        with pe.If(passes > 1):
            with pe.Fori(1, passes) as j:
                expert_pass(j)

    block.__exit__(None, None, None)


def stored(c, s):
    return sum(32 if SECTION[k][0] in ("k", "v") else 16 for k in range(c + 1) if k % 3 == s)


_INS = ["x_prompt", "x_sample", "cache_k", "cache_v", "state_ret", "g_mix", "w_in", "g_q", "g_k", "lambda_q1",
        "lambda_k1", "lambda_q2", "lambda_k2", "g_ret", "w_ret_o", "g_sub", "w_diff_o", "w_out", "g_ffn", "w_group",
        "b_group", "w_expert", "b_expert", "w_gate", "w_up", "w_down"]
_OUTS = {"y": (SINK + P, D_MODEL), "k_new": (REAL, D_MODEL), "v_new": (REAL, D_MODEL),
         "s_prompt": (H, DK, DV), "s_sample": (H, DK, DV)}


def kernel(**inputs):
    import concourse.bacc as bacc
    from concourse.bass_utils import run_bass_kernel_spmd

    nc = bacc.Bacc("TRN2", target_bir_lowering=False, num_devices=1)
    arrays, ins = {}, {}
    by_row = {"g_ffn_col": inputs["g_ffn"].reshape(KC, P).T}
    for name, arr in [(n, inputs[n]) for n in _INS] + list(by_row.items()) + list(shape_constants().items()):
        arr = np.ascontiguousarray(arr)
        arrays[f"in_{name}"] = arr
        ins[name] = nc.dram_tensor(f"in_{name}", arr.shape, mybir.dt.from_np(arr.dtype), kind="ExternalInput").ap()
    outs = {n: nc.dram_tensor(f"out_{n}", s, mybir.dt.float32, kind="ExternalOutput").ap() for n, s in _OUTS.items()}
    build(nc, ins, outs)
    r = run_bass_kernel_spmd(nc, [arrays], core_ids=[0]).results[0]
    y, k, v, s_p, s_s = (r[f"out_{n}"] for n in _OUTS)
    return (y[None, :PROMPT], y[None, PROMPT:REAL],
            k[:PROMPT].reshape(1, 1, PROMPT, H, DV), v[:PROMPT].reshape(1, 1, PROMPT, H, DV), s_p[None, None],
            k[PROMPT:].reshape(1, 1, SAMPLE, H, DV), v[PROMPT:].reshape(1, 1, SAMPLE, H, DV), s_s[None, None])
```
